# Optimizing a Trainium2 kernel written in Bass

```python
import jax, jax.numpy as jnp
from jax import lax
import numpy as np

D_MODEL = 2048
BATCH = 1
SEQ = 128
DEPTH = 2
DEC_BATCH = 1
DEC_SEQ = 128
PAST_LEN = 128

GRID_W = 64
HEAD_DIM = 128
H_A = 6
H_B = 6
KV_B = 2
REP_B = H_B // KV_B
G_C = 4
C_GROUP = 128
W_A = H_A * HEAD_DIM
W_B = H_B * HEAD_DIM
W_C = G_C * C_GROUP
MIX_WIDTH = W_A + W_B + W_C
NA_ROWS = 8
NA_COLS = 16
WIN = 128
BLK = 128
CHUNK = 128
D_FF = -(-8 * D_MODEL // (3 * 256)) * 256
N_MOD = 6
ROPE_BASE = 10000.0
NORM_EPS = 1e-6
ATTN_SCALE = HEAD_DIM ** -0.5
Q_A = 0
K_A = Q_A + W_A
V_A = K_A + W_A
Q_B = V_A + W_A
K_B = Q_B + W_B
V_B = K_B + KV_B * HEAD_DIM
U_C = V_B + KV_B * HEAD_DIM
V_C = U_C + W_C
IN_WIDTH = V_C + W_C

kernel_name = 'hybrid_prefix_diffusion_step'

def rms_norm(x, g):
    x32 = x.astype(jnp.float32)
    y = x32 * lax.rsqrt(jnp.mean(x32 * x32, axis=-1, keepdims=True) + NORM_EPS)
    return (y * g.astype(jnp.float32)).astype(x.dtype)

def layer_norm(x, g, b):
    x32 = x.astype(jnp.float32)
    mu = jnp.mean(x32, axis=-1, keepdims=True)
    xc = x32 - mu
    y = xc * lax.rsqrt(jnp.mean(xc * xc, axis=-1, keepdims=True) + NORM_EPS)
    return (y * g.astype(jnp.float32) + b.astype(jnp.float32)).astype(x.dtype)

def rope_1d(x, pos):
    half = x.shape[-1] // 2
    freqs = ROPE_BASE ** (-jnp.arange(half, dtype=jnp.float32) / half)
    ang = pos.astype(jnp.float32)[:, None] * freqs[None, :]
    cos, sin = jnp.cos(ang), jnp.sin(ang)
    x32 = x.astype(jnp.float32)
    x1, x2 = x32[..., :half], x32[..., half:]
    return jnp.concatenate([x1 * cos - x2 * sin, x1 * sin + x2 * cos], axis=-1).astype(x.dtype)

def axial_rope(x):
    n = x.shape[-2]
    t = jnp.arange(n)
    half = x.shape[-1] // 2
    return jnp.concatenate([rope_1d(x[..., :half], t // GRID_W),
                            rope_1d(x[..., half:], t % GRID_W)], axis=-1)

def modulation(cond, w_mod, b_mod):
    m = jax.nn.silu(cond) @ w_mod + b_mod
    return jnp.split(m[..., None, :], N_MOD, axis=-1)

def split_projection(h, w_in):
    z = h @ w_in
    b, L, _ = z.shape
    def heads(a, nh):
        return a.reshape(b, L, nh, HEAD_DIM).transpose(0, 2, 1, 3)
    q_a = heads(z[..., Q_A:K_A], H_A)
    k_a = heads(z[..., K_A:V_A], H_A)
    v_a = heads(z[..., V_A:Q_B], H_A)
    q_b = z[..., Q_B:K_B].reshape(b, L, KV_B, REP_B, HEAD_DIM).transpose(0, 2, 3, 1, 4)
    k_b = heads(z[..., K_B:V_B], KV_B)
    v_b = heads(z[..., V_B:U_C], KV_B)
    u_c = jax.nn.gelu(z[..., U_C:V_C])
    v_c = jax.nn.gelu(z[..., V_C:IN_WIDTH])
    return q_a, k_a, v_a, q_b, k_b, v_b, u_c, v_c

def merge_heads(o_a, o_b, o_c, w_out):
    b, _, L, _ = o_a.shape
    o_a = o_a.transpose(0, 2, 1, 3).reshape(b, L, W_A)
    o_b = o_b.transpose(0, 3, 1, 2, 4).reshape(b, L, W_B)
    return jnp.concatenate([o_a, o_b, o_c], axis=-1) @ w_out

def context_attention(q, k, v, sink):
    b, g, r, s, d = q.shape
    nq = s // BLK
    qb = jnp.moveaxis(q.reshape(b, g, r, nq, BLK, d), 3, 0)
    def block(qi):
        sc = jnp.einsum('bgrqd,bgkd->bgrqk', qi, k).astype(jnp.float32) * ATTN_SCALE
        if sink is not None:
            sk = jnp.broadcast_to(sink.astype(jnp.float32)[None, :, :, None, None], (b, g, r, BLK, 1))
            sc = jnp.concatenate([sc, sk], axis=-1)
        p = jax.nn.softmax(sc, axis=-1)[..., :s].astype(v.dtype)
        return jnp.einsum('bgrqk,bgkd->bgrqd', p, v)
    out = lax.map(block, qb)
    return jnp.moveaxis(out, 0, 3).reshape(b, g, r, s, d)

def neighbourhood_attention(q, k, v, ck, cv, rpb):
    b, h, n, d = q.shape
    rows = n // GRID_W
    kr = min(NA_ROWS, rows)
    r = jnp.arange(rows)
    row_idx = jnp.clip(r - kr // 2, 0, rows - kr)[:, None] + jnp.arange(kr)[None, :]
    col = jnp.arange(GRID_W)
    c0 = jnp.clip(col - NA_COLS // 2, 0, GRID_W - NA_COLS)
    col_ok = (col[None, :] >= c0[:, None]) & (col[None, :] < c0[:, None] + NA_COLS)
    idx_r = row_idx - r[:, None] + NA_ROWS - 1
    idx_c = jnp.clip(col[None, :] - col[:, None] + NA_COLS - 1, 0, 2 * NA_COLS - 2)
    bias = rpb[:, idx_r[:, None, :, None], idx_c[None, :, None, :]].astype(jnp.float32)
    q5 = q.reshape(b, h, rows, GRID_W, d)
    k_band = k.reshape(b, h, rows, GRID_W, d)[:, :, row_idx]
    v_band = v.reshape(b, h, rows, GRID_W, d)[:, :, row_idx]
    s_loc = jnp.einsum('bhrqd,bhrjkd->bhrqjk', q5, k_band).astype(jnp.float32) * ATTN_SCALE + bias[None]
    s_loc = jnp.where(col_ok[:, None, :], s_loc, -jnp.inf).reshape(b, h, rows, GRID_W, kr * GRID_W)
    s_ctx = jnp.einsum('bhrqd,bhsd->bhrqs', q5, ck).astype(jnp.float32) * ATTN_SCALE
    p = jax.nn.softmax(jnp.concatenate([s_loc, s_ctx], axis=-1), axis=-1).astype(v.dtype)
    p_loc = p[..., :kr * GRID_W].reshape(b, h, rows, GRID_W, kr, GRID_W)
    p_ctx = p[..., kr * GRID_W:]
    out = (jnp.einsum('bhrqjk,bhrjkd->bhrqd', p_loc, v_band)
           + jnp.einsum('bhrqs,bhsd->bhrqd', p_ctx, cv))
    return out.reshape(b, h, n, d)

def window_attention(q, k, v, ck, cv, sink):
    b, g, r, n, d = q.shape
    nb = n // BLK
    span = BLK + 2 * WIN
    pad = ((0, 0), (0, 0), (WIN, WIN), (0, 0))
    kp, vp = jnp.pad(k, pad), jnp.pad(v, pad)
    idx = (jnp.arange(nb) * BLK)[:, None] + jnp.arange(span)[None, :]
    kb, vb = kp[:, :, idx], vp[:, :, idx]
    qb = q.reshape(b, g, r, nb, BLK, d)
    qpos = jnp.arange(n).reshape(nb, BLK)
    kpos = idx - WIN
    ok = ((jnp.abs(qpos[:, :, None] - kpos[:, None, :]) <= WIN)
          & (kpos[:, None, :] >= 0) & (kpos[:, None, :] < n))
    s_loc = jnp.einsum('bgrnqd,bgnkd->bgrnqk', qb, kb).astype(jnp.float32) * ATTN_SCALE
    s_loc = jnp.where(ok, s_loc, -jnp.inf)
    s_ctx = jnp.einsum('bgrnqd,bgsd->bgrnqs', qb, ck).astype(jnp.float32) * ATTN_SCALE
    sk = jnp.broadcast_to(sink.astype(jnp.float32)[None, :, :, None, None, None], (b, g, r, nb, BLK, 1))
    p = jax.nn.softmax(jnp.concatenate([s_loc, s_ctx, sk], axis=-1), axis=-1).astype(v.dtype)
    sc = ck.shape[2]
    out = (jnp.einsum('bgrnqk,bgnkd->bgrnqd', p[..., :span], vb)
           + jnp.einsum('bgrnqs,bgsd->bgrnqd', p[..., span:span + sc], cv))
    return out.reshape(b, g, r, n, d)

def chunk_gmlp(u, v, w_s, b_s, ln_g, ln_b):
    b, L, _ = v.shape
    vn = layer_norm(v, ln_g, ln_b).reshape(b, L // CHUNK, CHUNK, G_C, C_GROUP)
    s = jnp.einsum('gpq,bnqgc->bnpgc', w_s, vn) + b_s.T[None, None, :, :, None]
    return u * s.reshape(b, L, W_C)

def ffn_sublayer(x, shift, scale, gate, g_pre, g_post, w_gate, w_up, w_down):
    h = rms_norm(x, g_pre) * (1 + scale) + shift
    f = (jax.nn.silu(h @ w_gate) * (h @ w_up)) @ w_down
    return x + gate * rms_norm(f, g_post)

def setup_inputs(seed: int = 0) -> dict:
    key = jax.random.key(seed)
    ks = jax.random.split(key, 26)
    def nrm(k, shape, s):
        return jax.random.normal(k, shape, jnp.float32) * s
    D = D_MODEL
    return {
        'x_prompt': nrm(ks[0], (BATCH, SEQ, D), 1.0),
        'x_sample': nrm(ks[1], (DEC_BATCH, DEC_SEQ, D), 1.0),
        'cache_a_k': nrm(ks[2], (DEC_BATCH, DEPTH, H_A, PAST_LEN, HEAD_DIM), 1.0),
        'cache_a_v': nrm(ks[3], (DEC_BATCH, DEPTH, H_A, PAST_LEN, HEAD_DIM), 1.0),
        'cache_b_k': nrm(ks[4], (DEC_BATCH, DEPTH, KV_B, PAST_LEN, HEAD_DIM), 1.0),
        'cache_b_v': nrm(ks[5], (DEC_BATCH, DEPTH, KV_B, PAST_LEN, HEAD_DIM), 1.0),
        'c': nrm(ks[6], (DEC_BATCH, D), 1.0),
        'c_ctx': nrm(ks[7], (D,), 1.0),
        'mod_w': nrm(ks[8], (DEPTH, D, N_MOD * D), 0.5 * D ** -0.5),
        'mod_b': nrm(ks[9], (DEPTH, N_MOD * D), 0.02),
        'norm_mix_pre': 1.0 + nrm(ks[10], (DEPTH, D), 0.05),
        'norm_mix_post': 1.0 + nrm(ks[11], (DEPTH, D), 0.05),
        'norm_ffn_pre': 1.0 + nrm(ks[12], (DEPTH, D), 0.05),
        'norm_ffn_post': 1.0 + nrm(ks[13], (DEPTH, D), 0.05),
        'w_in': nrm(ks[14], (DEPTH, D, IN_WIDTH), D ** -0.5),
        'w_out': nrm(ks[15], (DEPTH, MIX_WIDTH, D), MIX_WIDTH ** -0.5),
        'rpb_a': nrm(ks[16], (DEPTH, H_A, 2 * NA_ROWS - 1, 2 * NA_COLS - 1), 0.3),
        'sink_b': nrm(ks[17], (DEPTH, KV_B, REP_B), 1.0),
        'gmlp_ln_g': 1.0 + nrm(ks[18], (DEPTH, W_C), 0.05),
        'gmlp_ln_b': nrm(ks[19], (DEPTH, W_C), 0.02),
        'gmlp_w': nrm(ks[20], (DEPTH, G_C, CHUNK, CHUNK), CHUNK ** -0.5),
        'gmlp_b': 1.0 + nrm(ks[21], (DEPTH, G_C, CHUNK), 0.1),
        'w_gate': nrm(ks[22], (DEPTH, D, D_FF), D ** -0.5),
        'w_up': nrm(ks[23], (DEPTH, D, D_FF), D ** -0.5),
        'w_down': nrm(ks[24], (DEPTH, D_FF, D), D_FF ** -0.5),
    }

def reference(x_prompt, x_sample, cache_a_k, cache_a_v, cache_b_k, cache_b_v, c, c_ctx,
              mod_w, mod_b, norm_mix_pre, norm_mix_post, norm_ffn_pre, norm_ffn_post,
              w_in, w_out, rpb_a, sink_b, gmlp_ln_g, gmlp_ln_b, gmlp_w, gmlp_b,
              w_gate, w_up, w_down):
    xp = x_prompt
    ka_list, va_list, kb_list, vb_list = [], [], [], []
    for l in range(DEPTH):
        sm, cm, gm, sf, cf, gf = modulation(c_ctx, mod_w[l], mod_b[l])
        h = rms_norm(xp, norm_mix_pre[l]) * (1 + cm) + sm
        q_a, k_a, v_a, q_b, k_b, v_b, u_c, v_c = split_projection(h, w_in[l])
        o_a = context_attention(q_a[:, :, None], k_a, v_a, None)[:, :, 0]
        o_b = context_attention(q_b, k_b, v_b, sink_b[l])
        o_c = chunk_gmlp(u_c, v_c, gmlp_w[l], gmlp_b[l], gmlp_ln_g[l], gmlp_ln_b[l])
        xp = xp + gm * rms_norm(merge_heads(o_a, o_b, o_c, w_out[l]), norm_mix_post[l])
        xp = ffn_sublayer(xp, sf, cf, gf, norm_ffn_pre[l], norm_ffn_post[l], w_gate[l], w_up[l], w_down[l])
        ka_list.append(k_a)
        va_list.append(v_a)
        kb_list.append(k_b)
        vb_list.append(v_b)
    xs = x_sample
    for l in range(DEPTH):
        sm, cm, gm, sf, cf, gf = modulation(c, mod_w[l], mod_b[l])
        h = rms_norm(xs, norm_mix_pre[l]) * (1 + cm) + sm
        q_a, k_a, v_a, q_b, k_b, v_b, u_c, v_c = split_projection(h, w_in[l])
        o_a = neighbourhood_attention(q_a, k_a, v_a, cache_a_k[:, l], cache_a_v[:, l], rpb_a[l])
        o_b = window_attention(axial_rope(q_b), axial_rope(k_b), v_b,
                               cache_b_k[:, l], cache_b_v[:, l], sink_b[l])
        o_c = chunk_gmlp(u_c, v_c, gmlp_w[l], gmlp_b[l], gmlp_ln_g[l], gmlp_ln_b[l])
        xs = xs + gm * rms_norm(merge_heads(o_a, o_b, o_c, w_out[l]), norm_mix_post[l])
        xs = ffn_sublayer(xs, sf, cf, gf, norm_ffn_pre[l], norm_ffn_post[l], w_gate[l], w_up[l], w_down[l])
    new_a_k = jnp.stack(ka_list, axis=1)
    new_a_v = jnp.stack(va_list, axis=1)
    new_b_k = jnp.stack(kb_list, axis=1)
    new_b_v = jnp.stack(vb_list, axis=1)
    return (xp, xs, new_a_k, new_a_v, new_b_k, new_b_v)


_drawn_inputs = setup_inputs


def setup_inputs(seed=0):
    import zlib

    import numpy as np

    out = dict(_drawn_inputs(seed))
    spreads = {}
    factors = {'norm_mix_post': 2.707,
     'norm_ffn_post': 2.92,
     'rpb_a': 5.05,
     'sink_b': 8.0,
     'gmlp_ln_g': 4.256,
     'gmlp_ln_b': 8.0,
     'cache_b_k': 2.89}
    for name, (base, spread) in spreads.items():
        noise = np.random.default_rng([zlib.crc32(name.encode()), seed]).standard_normal(out[name].shape)
        drawn = base * np.exp(spread * noise) if base else spread * noise
        out[name] = __import__('jax').numpy.asarray(drawn.astype(out[name].dtype))
    for name, factor in factors.items():
        out[name] = (out[name] * factor).astype(out[name].dtype)
    return out
```

```python
from contextlib import ExitStack

import numpy as np

import concourse.bass as bass
from concourse import mybir

F32 = mybir.dt.float32
F32R = mybir.dt.float32r
ALU = mybir.AluOpType
ACT = mybir.ActivationFunctionType
AX_X = mybir.AxisListType.X

P = 128
D = 2048
KD = D // P
DEPTH = 2
CH = 512
ND = D // CH
NH = 6
KVB = 2
GC = 4
W_IN = 4608
W_INC = W_IN // CH
Q_A, K_A, V_A, Q_B, K_B, V_B, U_C, V_C = 0, 768, 1536, 2304, 3072, 3328, 3584, 4096
FF = 5632
FFC = FF // CH
GROUPS = [(0, 4), (4, 4), (8, 3)]
NMODC = 6 * D // CH
SCALE = float(P) ** -0.5
EPS = 1e-6
NEG = -1e30
GRID = 64

KB = 2
UNIT = KD // KB
RING = 4
LEAD = 4

MOD_INIT = 8
MOD_ATT = [4, 1]
MOD_PRE_FFN = [3, 0]
MOD_FFN = [True, False]
MOD_PRE_MIX = 3

BANKS = ["A0", "A1", "B0", "B1", "M", "X0", "X1", "T"]

def attention_steps(n_mods):
    s = [("turn", 0, b) for b in range(5)] + [("score", 0)] + [("turn_ws",)] + [("score", 1)]
    s += [("turn_ck", b) for b in range(2)] + [("mod",)] * (n_mods > 0)
    s += [("norm_v", 0), ("norm_v", 1)]
    s += [("turn", 1, b) for b in range(5)] + [("soft", 0), ("value", 0), ("score", 2)]
    s += [("mod",)] * (n_mods > 1)
    s += [("soft", 1), ("value", 1), ("score", 3), ("gate_c", 0), ("gate_c", 1)]
    s += [("mod",)] * (n_mods > 2)
    s += [("soft", 2), ("value", 2), ("turn_c", 0), ("turn_c", 1)]
    s += [("mod",)] * (n_mods > 3)
    s += [("soft", 3), ("value", 3)]
    return s


def score_banks(n):
    return [range(0, 4), range(4, 6)] if n < 2 else [range(0, 2), range(2, 4), range(4, 6)]


class Plan:

    def __init__(self):
        self.unit, self.mod, self.use = 0, 0, dict.fromkeys(BANKS, 0)
        self.fills, self.fill = dict.fromkeys(BANKS, 0), {}
        self.at = {}
        self.turn_bank = 0
        self.acc_bank = 0

        self.mark(("init",))
        self.take("X0")
        self.mods(MOD_INIT)
        for l in range(DEPTH):
            self.pre(l, 0)
            self.mark((l, "win"))
            self.unit += W_INC
            self.mods(W_INC)
            self.takes(["A0", "A1"], W_INC)
            self.attention(l)
            self.gate(l, 0)
            self.mark((l, "out"))
            self.unit += ND
            self.takes(["A0", "A1", "B0", "B1"], ND // 2)
            self.mark((l, "mod_pre_ffn"))
            self.mods(MOD_PRE_FFN[l])
            self.pre(l, 1)
            for g, (_, n) in enumerate(GROUPS):
                self.mark((l, "up", g))
                self.unit += 2 * n
                self.takes(["A0", "A1", "B0", "B1", "X0", "X1"], n)
                if MOD_FFN[l]:
                    self.mods(n)
                if g == 1:
                    self.gate(l, 1)
                self.mark((l, "down", g))
                self.unit += n if n < 4 else ND
                self.takes(["A0", "A1", "B0", "B1"], ND // 2)
            if l + 1 < DEPTH:
                self.mark((l, "mod_pre_mix"))
                self.mods(MOD_PRE_MIX)

    def mark(self, key):
        self.at[key] = (self.unit, self.mod, dict(self.use))

    def mods(self, n):
        self.unit += n
        self.mod += n
        self.takes(["M", "T"], n)

    def takes(self, banks, n):
        for b in banks:
            self.use[b] += n
            if b in ("X0", "X1", "T"):
                self.fills[b] += n

    def take(self, bank):
        self.use[bank] += 1
        self.fills[bank] += 1
        self.fill[(bank, self.use[bank] - 1)] = self.fills[bank]
        return bank, self.use[bank] - 1

    def turn(self):
        self.turn_bank ^= 1
        return self.take(("X0", "X1")[self.turn_bank])

    def acc(self):
        self.acc_bank = (self.acc_bank + 1) % 4
        return self.take(BANKS[self.acc_bank])

    def pre(self, l, which):
        self.mark((l, "pre", which))
        self.at[(l, "pre_uses", which)] = [[self.take(f"X{s}") for s in range(2)] for _ in range(KD // 4)]

    def gate(self, l, which):
        self.at[(l, "gate_uses", which)] = [[self.take(f"X{s}") for s in range(2)] for _ in range(ND)]

    def attention(self, l):
        uses = []
        for step in attention_steps(MOD_ATT[l]):
            mine = (self.unit, self.mod)
            banks = []
            if step[0] in ("turn", "turn_ck", "turn_ws", "turn_c"):
                banks = [self.turn()]
            elif step[0] == "score":
                banks = [self.acc() for _ in score_banks(step[1])]
            elif step[0] == "value":
                banks = [self.turn() for _ in range(2 if step[1] < 2 else 3)] + [self.acc() for _ in range(2)]
            elif step[0] == "gate_c":
                banks = [self.acc()]
            elif step[0] == "mod":
                self.mods(1)
            uses.append((step, banks, mine))
        self.at[(l, "attention")] = uses


def build_program(nc, a):
    plan = Plan()
    TOTAL = plan.unit * UNIT
    xin = [a["x_prompt"][0], a["x_sample"][0]]
    xout = [a["out_0"][0], a["out_1"][0]]

    with ExitStack() as ctx:
        def sem(name):
            return ctx.enter_context(nc.semaphore(name))

        def sb(name, shape, dt=F32, at=ctx):
            return at.enter_context(nc.sbuf_tensor(name, shape, dt))

        bank = {b: ctx.enter_context(nc.psum_tensor(f"bank_{b}", [P, CH], F32)) for b in BANKS}

        raw = sb("raw", [P, RING, KB, CH])
        whi = sb("whi", [P, RING, KB, CH], F32R)
        wlo = sb("wlo", [P, RING, KB, CH], F32R)
        x = sb("x", [P, 2, D])
        xt_hi = sb("xt_hi", [P, KD, 2 * P], F32R)
        xt_lo = sb("xt_lo", [P, KD, 2 * P], F32R)
        ident = sb("ident", [P, P])
        rsel = sb("rsel", [4, 2])
        rope = sb("rope", [P, 2, P])
        edge = sb("edge", [P, P])
        vrows = sb("vrows", [P, 4, P])
        vcols = sb("vcols", [P, 4 * P])
        silu_c = sb("silu_c", [P, 2, KD])
        cond = sb("cond", [P, KD * 4 + P], F32R)
        mrow = sb("mrow", [4, CH])
        modt = sb("modt", [P, DEPTH * NMODC * 8])
        shift = sb("shift", [P, KD, 2])
        scal = sb("scal", [P, KD, 2])
        gatev = sb("gatev", [P, KD, 2])
        ssq = sb("ssq", [P, 2, ND])
        ssx = sb("ssx", [P, 2, ND])
        ms = sb("ms", [P, 2])
        rstd = sb("rstd", [P, 2])
        minus_half = sb("minus_half", [P, 2])
        junk = sb("junk", [P, CH])

        ffn = ExitStack()
        gate = sb("gate", [P, 2, D], F32, ffn)
        ht_hi = sb("ht_hi", [P, KD, 2 * P], F32R, ffn)
        ht_lo = sb("ht_lo", [P, KD, 2 * P], F32R, ffn)
        f = sb("f", [P, 2, D], F32, ffn)
        hid = sb("hid", [P, 2, CH], F32, ffn)
        sil = sb("sil", [P, 2, CH], F32, ffn)
        xtmp = sb("xtmp", [P, 2, 4, P], F32, ffn)
        ffn.close()
        z = sb("z", [P, 2, W_IN])
        qkt = sb("qkt", [P, 20, P])
        ck = sb("ck", [P, NH + KVB, P])
        cv = sb("cv", [P, NH + KVB, P])
        ckt = sb("ckt", [P, NH + KVB, P])
        bias = sb("bias", [P, NH, P])
        turned_b = sb("turned_b", [P, 8, P])
        crossed = sb("crossed", [P, 8, P])
        prob = sb("prob", [P, 2, NH, 2 * P])
        pt = sb("pt", [P, 12, P])
        ln_g = sb("ln_g", [P, CH])
        ln_b = sb("ln_b", [P, CH])
        ws = sb("ws", [P, GC, P])
        wst = sb("wst", [P, GC, P])
        sink = sb("sink", [P, NH])
        nsink = sb("nsink", [P, NH])
        msum = sb("msum", [P, 2])
        clear = sb("clear", [P, len(BANKS)])
        rmax = sb("rmax", [P, 4, NH])
        nmax = sb("nmax", [P, 4, NH])
        den = sb("den", [P, 4, NH])
        esink = sb("esink", [P, 4, NH])
        vstat = sb("vstat", [P, 2, 6])
        vmv = sb("vmv", [P, 2, 2])
        vrstd = sb("vrstd", [P, 2])

        PADW = 2 * GRID - 1
        rpb_pad = nc.dram_tensor("rpb_pad", [DEPTH * NH * 3, PADW], F32, kind="Internal").ap()
        rpb_rows = nc.dram_tensor("rpb_rows", [GRID, DEPTH * NH * 3, PADW], F32, kind="Internal").ap()

        filled = {b: sem(f"filled_{b}") for b in BANKS}
        freed = {b: sem(f"freed_{b}") for b in BANKS}
        raw_landed = [sem(f"raw_landed_{i}") for i in range(RING)]
        hi_ready = sem("hi_ready")
        lo_ready = sem("lo_ready")
        w_used = sem("w_used")
        const_loaded = sem("const_loaded")
        x_loaded = sem("x_loaded")
        pad_cleared = sem("pad_cleared")
        pad_filled = sem("pad_filled")
        pad_copied = sem("pad_copied")
        att_loaded = sem("att_loaded")
        vrows_clear = sem("vrows_clear")
        silu_ready = sem("silu_ready")
        cond_ready = sem("cond_ready")
        dve_own = sem("dve_own")
        act_own = sem("act_own")
        pool_own = sem("pool_own")
        mrow_ready = sem("mrow_ready")
        xt_ready = sem("xt_ready")
        vec_ready = sem("vec_ready")
        sq_ready = sem("sq_ready")
        ms_ready = sem("ms_ready")
        rstd_ready = sem("rstd_ready")
        xn_ready = sem("xn_ready")
        gate_ready = sem("gate_ready")
        hi_x = sem("hi_x")
        x_new = sem("x_new")
        ht_hi_ready = sem("ht_hi_ready")
        gelu_ready = sem("gelu_ready")
        rope_ready = sem("rope_ready")
        nm_ready = sem("nm_ready")
        exp_ready = sem("exp_ready")
        pn_ready = sem("pn_ready")
        vmv_ready = sem("vmv_ready")
        vrstd_ready = sem("vrstd_ready")
        vn_ready = sem("vn_ready")
        kv_stored = sem("kv_stored")
        x_stored = sem("x_stored")

        def vec(v, l):
            c = (v * DEPTH + l) * KD
            return vcols[:, c:c + KD].unsqueeze(2).broadcast_to([P, KD, 2])

        def mod_b(l, v):
            c = P * (1 + l) + v * KD
            return vcols[:, c:c + KD].unsqueeze(2).broadcast_to([P, KD, 2])

        def mod_t(l, v):
            c = (l * 6 + v) * KD * 2
            return modt[:, c:c + KD * 2].rearrange("p (t c) -> p t c", c=2)

        def mod_done(l, v):
            return l * NMODC + (v + 1) * ND

        def four(ap):
            return ap.rearrange("p (t c) -> p t c", t=4)

        def xt_count(l, which):
            return 16 * l + 8 * (which + 1)

        N_CONST = 13
        N_ATT = 12

        block = ctx.enter_context(nc.Block())

        @block.sync
        def _(sp):
            def piece(u, ph, src):
                if not (isinstance(u, int) and u * UNIT + ph < RING):
                    sp.wait_ge(lo_ready, u * UNIT + (ph - RING + 1))
                sp.dma_start(raw[:, ph % RING], src.rearrange("(t p) n -> p t n", p=P)).then_inc(
                    raw_landed[ph % RING], 16)

            def chunk(u, w, row0, col, pieces=UNIT, ph=0):
                for j in range(pieces):
                    piece(u, ph + j, w[row0 + j * KB * P:row0 + (j + 1) * KB * P, bass.ds(col, CH)])

            def mod_chunk(u, m, l):
                chunk(u, a["mod_w"][l], 0, (m - l * NMODC) * CH)

            u, m, _ = plan.at[("init",)]
            mod_chunk(u, m, 0)
            with sp.Fori(1, MOD_INIT) as i:
                mod_chunk(i + u, i + m, 0)
            for l in range(DEPTH):
                u, m, _ = plan.at[(l, "win")]
                with sp.Fori(0, W_INC) as i:
                    mod_chunk(i * 2 + u, i + m, l)
                    chunk(i * 2 + (u + 1), a["w_in"][l], 0, i * CH)
                for step, _, (u, m) in plan.at[(l, "attention")]:
                    if step[0] == "mod":
                        mod_chunk(u, m, l)
                u, _, _ = plan.at[(l, "out")]
                with sp.Fori(0, ND) as i:
                    chunk(i + u, a["w_out"][l], 0, i * CH)
                u, m, _ = plan.at[(l, "mod_pre_ffn")]
                for i in range(MOD_PRE_FFN[l]):
                    mod_chunk(u + i, m + i, l)
                for g, (c0, n) in enumerate(GROUPS):
                    u, m, _ = plan.at[(l, "up", g)]
                    k = 3 if MOD_FFN[l] else 2
                    chunk(u, a["w_gate"][l], 0, c0 * CH)
                    with sp.Fori(0, n - 1) as i:
                        chunk(i * k + (u + 1), a["w_up"][l], 0, i * CH + c0 * CH)
                        chunk(i * k + (u + 2), a["w_gate"][l], 0, i * CH + (c0 + 1) * CH)
                        if MOD_FFN[l]:
                            mod_chunk(i * k + (u + 3), i + m, l + 1)
                    chunk(u + (n - 1) * k + 1, a["w_up"][l], 0, (c0 + n - 1) * CH)
                    if MOD_FFN[l]:
                        mod_chunk(u + n * k - 1, m + n - 1, l + 1)
                    u, _, _ = plan.at[(l, "down", g)]
                    if n == 4:
                        with sp.Fori(0, ND) as i:
                            chunk(i + u, a["w_down"][l], c0 * CH, i * CH)
                    else:
                        for i in range(ND):
                            chunk(u, a["w_down"][l], c0 * CH, i * CH, 2 * n, 2 * n * i)
                if l + 1 < DEPTH:
                    u, m, _ = plan.at[(l, "mod_pre_mix")]
                    for i in range(MOD_PRE_MIX):
                        mod_chunk(u + i, m + i, l + 1)
            sp.wait_ge(kv_stored, 16 * 4 * DEPTH)
            sp.wait_ge(x_stored, 32)

        @block.gpsimd
        def _(pool):
            own = [0]

            def link(ins):
                own[0] += 1
                ins.then_inc(pool_own, 1)
                pool.wait_ge(pool_own, own[0])

            def load(dst, src, s):
                pool.dma_start(dst, src).then_inc(s, 16)

            for s in range(2):
                load(x[:, s, :], xin[s], x_loaded)
            pool.wait_ge(vrows_clear, 1)
            for v, name in enumerate(["norm_mix_pre", "norm_mix_post", "norm_ffn_pre", "norm_ffn_post"]):
                load(vrows[v * 32:v * 32 + 32, 0, :], a[name].rearrange("l (t p) -> (l t) p", p=P), const_loaded)
            for l in range(DEPTH):
                load(vrows[0:96, 1 + l, :], a["mod_b"][l].rearrange("(t p) -> t p", p=P), const_loaded)
            load(vrows[0:16, 3, :], a["c_ctx"].rearrange("(t p) -> t p", p=P), const_loaded)
            load(vrows[16:32, 3, :], a["c"][0].rearrange("(t p) -> t p", p=P), const_loaded)
            load(vrows[32:40, 3, :], a["gmlp_b"].rearrange("l g p -> (l g) p"), const_loaded)
            load(ident[:], a["c_ident"], const_loaded)
            load(rsel[:], a["c_rsel"], const_loaded)
            load(rope[:], a["c_rope"].rearrange("p (a b) -> p a b", a=2), const_loaded)
            load(edge[:], a["c_edge"], const_loaded)
            load(rpb_pad, a["c_zero"], pad_cleared)
            pool.wait_ge(pad_cleared, 16)
            load(rpb_pad[:, GRID - 16:GRID + 15].rearrange("(g r) c -> g r c", r=3),
                 a["rpb_a"].rearrange("l h r c -> (l h) r c")[:, 6:9, :], pad_filled)
            pool.wait_ge(pad_filled, 16)
            load(rpb_rows, rpb_pad.unsqueeze(0).broadcast_to([GRID, DEPTH * NH * 3, PADW]), pad_copied)
            pool.wait_ge(pad_copied, 16)

            def power(src, dst, s_in, n_in, s_out):
                pool.wait_ge(s_in, n_in)
                pool.tensor_tensor(dst, src, minus_half[:, 0:dst.shape[-1]], ALU.pow).then_inc(s_out, 1)

            n_rstd = 0
            for l in range(DEPTH):
                n_rstd += 1
                power(ms[:], rstd[:], ms_ready, n_rstd, rstd_ready)
                pool.wait_ge(xt_ready, xt_count(l, 0))
                load(ck[:, 0:NH, :], a["cache_a_k"][0, l].rearrange("h k d -> k h d"), att_loaded)
                load(ck[:, NH:, :], a["cache_b_k"][0, l].rearrange("h k d -> k h d"), att_loaded)
                load(cv[:, 0:NH, :], a["cache_a_v"][0, l].rearrange("h k d -> k h d"), att_loaded)
                load(cv[:, NH:, :], a["cache_b_v"][0, l].rearrange("h k d -> k h d"), att_loaded)
                load(ln_g[:], a["gmlp_ln_g"][l:l + 1, :].broadcast_to([P, CH]), att_loaded)
                load(ln_b[:], a["gmlp_ln_b"][l:l + 1, :].broadcast_to([P, CH]), att_loaded)
                load(ws[:], a["gmlp_w"][l].rearrange("g p q -> p g q"), att_loaded)
                load(sink[:], a["sink_b"][l:l + 1].rearrange("l g r -> l (g r)").broadcast_to([P, NH]), att_loaded)
                for qr in range(2):
                    for kr in range(2):
                        first = (l * NH * 3 + kr - qr + 1) * PADW + GRID - 1
                        src = bass.AP(rpb_rows.tensor, first,
                                      [[DEPTH * NH * 3 * PADW - 1, GRID], [3 * PADW, NH], [1, GRID]])
                        load(bias[qr * GRID:(qr + 1) * GRID, :, kr * GRID:(kr + 1) * GRID], src, att_loaded)
                _, _, use = plan.at[(l, "win")]
                for b in ("A0", "A1"):
                    pool.wait_ge(freed[b], use[b] + W_INC + 1)
                zb = z[:, 1, Q_B:V_B].rearrange("p (h c) -> p h c", c=P)
                z5 = z[:, 1, Q_B:V_B].rearrange("p (h i c) -> p h i c", i=2, c=32)
                c5 = crossed[:].rearrange("p h c -> p (h c)").rearrange("p (h i c) -> p h i c", i=2, c=32)
                sn = rope[:, 1, :].rearrange("p (j i c) -> p j i c", j=2, i=2)
                pool.wait_ge(const_loaded, 16 * N_CONST)
                pool.tensor_tensor(turned_b[:], zb, rope[:, 0:1, :].broadcast_to([P, 8, P]), ALU.mult).then_inc(pool_own, 1)
                for i in range(2):
                    for j in range(2):
                        ins = pool.tensor_tensor(c5[:, j::2, i, :], z5[:, j::2, 1 - i, :],
                                                 sn[:, j:j + 1, i, :].broadcast_to([P, 8, 32]), ALU.mult)
                        ins.then_inc(pool_own, 1)
                own[0] += 5
                pool.wait_ge(pool_own, own[0])
                pool.tensor_tensor(turned_b[:], turned_b[:], crossed[:], ALU.add).then_inc(rope_ready, 1)
                for dst, col, n in ((a["out_2"], K_A, NH), (a["out_3"], V_A, NH), (a["out_4"], K_B, KVB), (a["out_5"], V_B, KVB)):
                    pool.dma_start(dst[0, l].rearrange("h t d -> t h d"),
                                   z[:, 0, col:col + n * P].rearrange("p (h c) -> p h c", c=P)).then_inc(kv_stored, 16)
                for s in range(2):
                    power(vmv[:, s, 1:2], vrstd[:, s:s + 1], vmv_ready, 2 * l + s + 1, vrstd_ready)
                for _ in range(3):
                    n_rstd += 1
                    power(ms[:], rstd[:], ms_ready, n_rstd, rstd_ready)
            for s in range(2):
                pool.wait_ge(x_new, 16 * DEPTH)
                pool.dma_start(xout[s], x[:, s, :]).then_inc(x_stored, 16)

        @block.tensor
        def _(pe):
            def free(b, i):
                pe.wait_ge(freed[b], i + 1)

            def read(b, i):
                pe.wait_ge(freed[b], i + 2)

            def dense(u, pair, i, hi, lo, nk=KD, ph=0, ready=None):
                free(pair + "0", i)
                free(pair + "1", i)
                for j in range(nk // KB):
                    pe.wait_ge(lo_ready, u * UNIT + (ph + j + 1))
                    slot = (ph + j) % RING
                    for kb in range(KB):
                        k = j * KB + kb
                        if ready:
                            ready(k)
                        for s in range(2):
                            t = slice(s * P, (s + 1) * P)
                            for n, (xs, ws_) in enumerate([(lo, whi), (hi, wlo), (hi, whi)]):
                                mm = pe.matmul(bank[f"{pair}{s}"][:], xs[:, k, t], ws_[:, slot, kb, :],
                                               start=(k == 0 and n == 0), stop=(k == nk - 1 and n == 2))
                    mm.then_inc(w_used, 1)

            def mod(u):
                for j in range(UNIT):
                    pe.wait_ge(lo_ready, u * UNIT + (j + 1))
                    for kb in range(KB):
                        k = j * KB + kb
                        st = cond[:, 4 * k:4 * k + P]
                        pe.matmul(bank["M"][:], st, wlo[:, j % RING, kb, :], start=(k == 0), stop=False)
                        mm = pe.matmul(bank["M"][:], st, whi[:, j % RING, kb, :], start=False, stop=(k == KD - 1))
                    mm.then_inc(w_used, 1)

            def mod_tail(i):
                pe.wait_ge(mrow_ready, i + 1)
                free("T", i)
                for t in range(4):
                    mm = pe.matmul(bank["T"][:, 2 * t:2 * t + 2], mrow[:, t * P:(t + 1) * P], rsel[:],
                                   start=True, stop=True)
                mm.then_inc(filled["T"], 1)

            def turn(b, i, tiles, skip_free=False):
                free(b, i)
                for n, t in enumerate(tiles):
                    mm = pe.transpose(bank[b][:, n * P:(n + 1) * P], t, ident[:])
                mm.then_inc(filled[b], 1)

            def pre(l, which):
                for b, uses in enumerate(plan.at[(l, "pre_uses", which)]):
                    for s, (bk, i) in enumerate(uses):
                        pe.wait_ge(xn_ready, 4 * l + 2 * which + s + 1)
                        turn(bk, i, [f[:, s, (4 * b + t) * P:(4 * b + t + 1) * P] for t in range(4)])

            def xt_ready_at(l, which):
                def ready(k):
                    if k % 4 == 0:
                        pe.wait_ge(xt_ready, xt_count(l, which) - 8 + 2 * (k // 4 + 1))
                return ready

            def gates(l, which):
                pe.wait_ge(gate_ready, 2 * l + which + 1)
                for n, uses in enumerate(plan.at[(l, "gate_uses", which)]):
                    for s, (bk, i) in enumerate(uses):
                        turn(bk, i, [gatev[:, 4 * n + t, s:s + 1].broadcast_to([P, P]) for t in range(4)])

            def attention(l):
                got = {}
                for step, banks, (u, m) in plan.at[(l, "attention")]:
                    kind = step[0]
                    if kind == "mod":
                        mod(u)
                        mod_tail(m)
                    elif kind == "turn":
                        s, b = step[1:]
                        if s == 1 and b == 3:
                            pe.wait_ge(rope_ready, l + 1)
                        turn(*banks[0], [z[:, s, h * P:(h + 1) * P] if h < 12 else
                                         turned_b[:, h - 12, :] if s else z[:, 0, Q_B + (h - 12) * P:Q_B + (h - 11) * P]
                                         for h in range(4 * b, 4 * b + 4)])
                    elif kind == "turn_ck":
                        b = step[1]
                        pe.wait_ge(att_loaded, 16 * N_ATT * (l + 1))
                        turn(*banks[0], [ck[:, h, :] for h in range(4 * b, 4 * b + 4)])
                    elif kind == "turn_ws":
                        pe.wait_ge(att_loaded, 16 * N_ATT * (l + 1))
                        turn(*banks[0], [ws[:, g, :] for g in range(GC)])
                    elif kind == "score":
                        n = step[1]
                        s, ty = divmod(n, 2)
                        for b, i in [got[("turn", s, j)][0] for j in range(5)] + [got[("turn_ck", j)][0] for j in range(2 * s)]:
                            read(b, i)
                        for (b, i), heads in zip(banks, score_banks(n)):
                            free(b, i)
                            for j, h in enumerate(heads):
                                q, k, c = (h, 6 + h, h) if ty == 0 else (12 + h, 18 + h // 3, 6 + h // 3)
                                o = j * P * (1 + s)
                                mm = pe.matmul(bank[b][:, o:o + P], qkt[:, q, :], qkt[:, k, :], start=True, stop=True)
                                if s:
                                    mm = pe.matmul(bank[b][:, o + P:o + 2 * P], qkt[:, q, :], ckt[:, c, :],
                                                   start=True, stop=True)
                            mm.then_inc(filled[b], 1)
                    elif kind == "value":
                        n = step[1]
                        s, ty = divmod(n, 2)
                        pe.wait_ge(pn_ready, 4 * l + n + 1)
                        blocks = [prob[:, n % 2, h, w * P:(w + 1) * P] for h in range(NH) for w in range(1 + s)]
                        turns, outs = banks[:-2], banks[-2:]
                        for j, (b, i) in enumerate(turns):
                            turn(b, i, blocks[4 * j:4 * j + 4])
                        for b, i in turns:
                            read(b, i)
                        for (b, i), heads in zip(outs, (range(0, 4), range(4, 6))):
                            free(b, i)
                            for j, h in enumerate(heads):
                                kv = h if ty == 0 else 6 + h // 3
                                col = V_A + h * P if ty == 0 else V_B + (h // 3) * P
                                vs = [z[:, s, col:col + P]] + s * [cv[:, kv, :]]
                                for w, v in enumerate(vs):
                                    mm = pe.matmul(bank[b][:, j * P:(j + 1) * P], v, pt[:, h * (1 + s) + w, :],
                                                   start=(w == 0), stop=(w == s))
                            mm.then_inc(filled[b], 1)
                    elif kind == "gate_c":
                        s = step[1]
                        pe.wait_ge(vn_ready, 2 * l + s + 1)
                        read(*got[("turn_ws",)][0])
                        b, i = banks[0]
                        free(b, i)
                        for g in range(GC):
                            mm = pe.matmul(bank[b][:, g * P:(g + 1) * P], wst[:, g, :],
                                           z[:, s, V_C + g * P:V_C + (g + 1) * P], start=True, stop=True)
                        mm.then_inc(filled[b], 1)
                    elif kind == "turn_c":
                        s = step[1]
                        read(*got[("gate_c", s)][0])
                        turn(*banks[0], [z[:, s, U_C + g * P:U_C + (g + 1) * P] for g in range(GC)])
                    got[step] = banks
                return got

            pe.wait_ge(const_loaded, 16 * N_CONST)
            pe.wait_ge(freed["X0"], 1)
            for t in range(4):
                mm = pe.transpose(bank["X0"][:, t * P:(t + 1) * P], vrows[:, t, :], ident[:])
            mm.then_inc(filled["X0"], 1)
            pe.wait_ge(cond_ready, 1)
            u, m, _ = plan.at[("init",)]
            with pe.Fori(0, MOD_INIT) as i:
                mod(i + u)
                mod_tail(i + m)
            for l in range(DEPTH):
                pre(l, 0)
                u, m, use = plan.at[(l, "win")]
                with pe.Fori(0, W_INC) as i:
                    mod(i * 2 + u)
                    dense(i * 2 + (u + 1), "A", i + use["A0"], xt_hi, xt_lo, ready=xt_ready_at(l, 0))
                    mod_tail(i + m)
                for b in ("A0", "A1"):
                    read(b, use[b] + W_INC - 1)
                got = attention(l)
                gates(l, 0)
                u, _, use = plan.at[(l, "out")]
                for step, banks in got.items():
                    if step[0] in ("value", "turn_c"):
                        for b, i in banks[-2:]:
                            read(b, i)
                with pe.Fori(0, ND // 2) as i:
                    dense(i * 2 + u, "A", i + use["A0"], xt_hi, xt_lo)
                    dense(i * 2 + (u + 1), "B", i + use["B0"], xt_hi, xt_lo)
                u, m, _ = plan.at[(l, "mod_pre_ffn")]
                for i in range(MOD_PRE_FFN[l]):
                    mod(u + i)
                    mod_tail(m + i)
                pre(l, 1)
                for g, (c0, n) in enumerate(GROUPS):
                    u, m, use = plan.at[(l, "up", g)]
                    k = 3 if MOD_FFN[l] else 2
                    xr = xt_ready_at(l, 1)

                    def turn_hidden(i):
                        for s in range(2):
                            read(f"B{s}", i + use[f"B{s}"])
                            turn(f"X{s}", i + use[f"X{s}"], [hid[:, s, t * P:(t + 1) * P] for t in range(4)])

                    dense(u, "A", use["A0"], xt_hi, xt_lo, ready=xr)
                    with pe.Fori(0, n - 1) as i:
                        dense(i * k + (u + 1), "B", i + use["B0"], xt_hi, xt_lo)
                        dense(i * k + (u + 2), "A", i + (use["A0"] + 1), xt_hi, xt_lo)
                        if MOD_FFN[l]:
                            mod(i * k + (u + 3))
                        turn_hidden(i)
                        if MOD_FFN[l]:
                            mod_tail(i + m)
                    dense(u + (n - 1) * k + 1, "B", use["B0"] + n - 1, xt_hi, xt_lo)
                    if MOD_FFN[l]:
                        mod(u + n * k - 1)
                    turn_hidden(n - 1)
                    if MOD_FFN[l]:
                        mod_tail(m + n - 1)
                    if g == 1:
                        gates(l, 1)

                    def hidden_ready(k):
                        if k % 4 == 0:
                            for s in range(2):
                                read(f"X{s}", use[f"X{s}"] + k // 4)

                    u, _, use2 = plan.at[(l, "down", g)]
                    if n == 4:
                        with pe.Fori(0, ND // 2) as i:
                            dense(i * 2 + u, "A", i + use2["A0"], ht_hi, ht_lo, ready=hidden_ready)
                            dense(i * 2 + (u + 1), "B", i + use2["B0"], ht_hi, ht_lo)
                    else:
                        for i in range(ND):
                            p = "AB"[i % 2]
                            dense(u, p, use2[p + "0"] + i // 2, ht_hi, ht_lo, nk=4 * n, ph=2 * n * i, ready=hidden_ready)
                if l + 1 < DEPTH:
                    u, m, _ = plan.at[(l, "mod_pre_mix")]
                    for i in range(MOD_PRE_MIX):
                        mod(u + i)
                        mod_tail(m + i)

        def ahead(split, u, ph=0, pieces=UNIT):
            for j in range(pieces):
                split(u, ph + LEAD + j)

        def past_end(u, ph):
            return isinstance(u, int) and u * UNIT + ph >= TOTAL

        @block.scalar
        def _(act):
            n_sq = [0]
            n_hi = [0]

            def split(u, ph):
                if past_end(u, ph):
                    return
                act.wait_ge(raw_landed[ph % RING], u * (16 * UNIT // RING) + 16 * (ph // RING + 1))
                if not (isinstance(u, int) and u * UNIT + ph < RING):
                    act.wait_ge(w_used, u * UNIT + (ph - RING + 1))
                act.copy(whi[:, ph % RING], raw[:, ph % RING]).then_inc(hi_ready, 1)

            def fill_of(b, i):
                act.wait_ge(filled[b], plan.fill.get((b, i), i + 1) if isinstance(i, int) else i + 1)

            def square(src, dst):
                if n_sq[0]:
                    act.wait_ge(sq_ready, n_sq[0])
                n_sq[0] += 1
                act.activation(junk[:], src, ACT.Square, accum_out=dst).then_inc(sq_ready, 1)

            def high(dst, src):
                n_hi[0] += 1
                act.copy(dst, src).then_inc(hi_x, 1)

            def mod_row(u, i):
                act.wait_ge(w_used, u * UNIT + UNIT)
                if not (isinstance(i, int) and i == 0):
                    act.wait_ge(filled["T"], i)
                act.copy(mrow[:], bank["M"][0:4, :]).then_inc(mrow_ready, 1)

            def mod(u, i):
                ahead(split, u)
                mod_row(u, i)

            def pre(l, which):
                j = 4 * l + 2 * which + 1
                if which == 0 and l == 0:
                    act.wait_ge(x_loaded, 32)
                for n in range(ND):
                    for s in range(2):
                        if j > 1:
                            act.wait_ge(x_new, 16 * l - 8 * (1 - which) + 2 * n + s + 1)
                        square(x[:, s, n * CH:(n + 1) * CH], ssx[:, s, n:n + 1])
                act.wait_ge(vec_ready, 2 * l + which + 1)
                for b, uses in enumerate(plan.at[(l, "pre_uses", which)]):
                    bk, i = uses[1]
                    fill_of(bk, i)
                    if b:
                        act.wait_ge(xt_ready, xt_count(l, which) - 8 + 2 * b)
                    for t in range(4):
                        k = 4 * b + t
                        ins = act.activation(xtmp[:, 1, t, :], bank[bk][:, t * P:(t + 1) * P], ACT.Identity,
                                             scale=scal[:, k, 1:2], bias=shift[:, k, 1:2])
                    ins.then_inc(freed[bk], 1)
                    for s, (bk, i) in enumerate(uses):
                        act.wait_ge(freed[bk], i + 2)
                        high(xt_hi[:, 4 * b:4 * b + 4, s * P:(s + 1) * P], xtmp[:, s])

            def gates(l, which):
                if which == 0:
                    act.wait_ge(kv_stored, 16 * 4 * (l + 1))
                for n, uses in enumerate(plan.at[(l, "gate_uses", which)]):
                    bk, i = uses[0]
                    fill_of(bk, i)
                    act.copy(gate[:, 0, n * CH:(n + 1) * CH], bank[bk][:]).then_inc(freed[bk], 1)

            def attention(l):
                for s in range(2):
                    if s == 0:
                        _, _, use = plan.at[(l, "win")]
                        for b in ("A0", "A1"):
                            act.wait_ge(freed[b], use[b] + W_INC + 1)
                    act.activation(z[:, s, U_C:W_IN], z[:, s, U_C:W_IN], ACT.Gelu_apprx_tanh).then_inc(gelu_ready, 1)
                for step, banks, (u, m) in plan.at[(l, "attention")]:
                    kind = step[0]
                    if kind == "mod":
                        mod(u, m)
                    elif kind in ("turn", "turn_ck", "turn_ws"):
                        b, i = banks[0]
                        dst = {"turn": qkt, "turn_ck": ckt, "turn_ws": wst}[kind]
                        j = step[-1] if kind != "turn_ws" else 0
                        if b == "X0":
                            fill_of(b, i)
                            act.copy(dst[:, 4 * j:4 * j + 4, :], four(bank[b][:])).then_inc(freed[b], 1)
                    elif kind == "score":
                        n = step[1]
                        s, ty = divmod(n, 2)
                        w = P * (1 + s)
                        act.wait_ge(nm_ready, 4 * l + n + 1)
                        for (b, i), heads in zip(banks, score_banks(n)):
                            for j, h in enumerate(heads):
                                dst = prob[:, n % 2, h, 0:w]
                                src = dst if n == 2 else bank[b][:, j * w:(j + 1) * w]
                                ins = act.activation(dst, src, ACT.Exp, bias=nmax[:, n, h:h + 1],
                                                     scale=1.0 if n == 2 else SCALE, accum_out=den[:, n, h:h + 1])
                            if n != 2:
                                ins.then_inc(freed[b], 1)
                        if ty:
                            ins = act.activation(esink[:, n, :], esink[:, n, :], ACT.Exp)
                        ins.then_inc(exp_ready, 1) if ty or n == 2 else exp_last(n)
                    elif kind == "value":
                        n = step[1]
                        s, ty = divmod(n, 2)
                        for j, (b, i) in enumerate(banks[:-2]):
                            if b == "X0":
                                fill_of(b, i)
                                k = min(4, NH * (1 + s) - 4 * j)
                                act.copy(pt[:, 4 * j:4 * j + k, :], four(bank[b][:])[:, 0:k, :]).then_inc(freed[b], 1)
                        for (b, i), heads in zip(banks[-2:], (range(0, 4), range(4, 6))):
                            fill_of(b, i)
                            k = len(heads)
                            k0 = ty * NH + heads[0]
                            high(xt_hi[:, k0:k0 + k, s * P:(s + 1) * P], four(bank[b][:])[:, 0:k, :])
                    elif kind == "turn_c":
                        s = step[1]
                        b, i = banks[0]
                        fill_of(b, i)
                        high(xt_hi[:, 12:16, s * P:(s + 1) * P], four(bank[b][:]))

            def exp_last(n):
                act.activation(esink[:, n, 0:1], nmax[:, n, 0:1], ACT.Copy).then_inc(exp_ready, 1)

            for j in range(LEAD):
                split(0, j)
            act.wait_ge(freed["X0"], 2)
            act.activation(silu_c[:].rearrange("p c t -> p (c t)"), vcols[:, 3 * P:3 * P + 2 * KD],
                           ACT.Silu).then_inc(silu_ready, 1)
            u, m, _ = plan.at[("init",)]
            mod(u, m)
            with act.Fori(1, MOD_INIT) as i:
                mod(i + u, i + m)
            for l in range(DEPTH):
                pre(l, 0)
                u, m, _ = plan.at[(l, "win")]
                with act.Fori(0, W_INC) as i:
                    mod(i * 2 + u, i + m)
                    ahead(split, i * 2 + (u + 1))
                attention(l)
                gates(l, 0)
                u, _, use = plan.at[(l, "out")]
                for i in range(ND):
                    ahead(split, u + i)
                    act.wait_ge(w_used, (u + i + 1) * UNIT)
                    for s in range(2):
                        b = f"{'AB'[i % 2]}{s}"
                        act.copy(f[:, s, i * CH:(i + 1) * CH], bank[b][:]).then_inc(freed[b], 1)
                    for s in range(2):
                        b = f"{'AB'[i % 2]}{s}"
                        act.wait_ge(freed[b], use[b] + i // 2 + 2)
                        square(f[:, s, i * CH:(i + 1) * CH], ssq[:, s, i:i + 1])
                u, m, _ = plan.at[(l, "mod_pre_ffn")]
                for i in range(MOD_PRE_FFN[l]):
                    mod(u + i, m + i)
                pre(l, 1)
                for g, (c0, n) in enumerate(GROUPS):
                    u, m, use = plan.at[(l, "up", g)]
                    k = 3 if MOD_FFN[l] else 2

                    def silu(u, i, first=False):
                        act.wait_ge(w_used, u * UNIT + UNIT)
                        if not (first and g == 0 and l == 0):
                            act.wait_ge(freed["B1"], i + (use["B1"] + 1))
                        for s in range(2):
                            act.activation(sil[:, s, :], bank[f"A{s}"][:], ACT.Silu).then_inc(freed[f"A{s}"], 1)

                    def hidden_high(i):
                        for s in range(2):
                            act.wait_ge(filled[f"X{s}"], i + (use[f"X{s}"] + 1))
                            act.wait_ge(x_loaded, 32)
                            act.copy(ht_hi[:, bass.ds(i * 4, 4), s * P:(s + 1) * P],
                                     four(bank[f"X{s}"][:])).then_inc(ht_hi_ready, 1)

                    ahead(split, u)
                    silu(u, 0, True)
                    with act.Fori(0, n - 1) as i:
                        ahead(split, i * k + (u + 1))
                        ahead(split, i * k + (u + 2))
                        silu(i * k + (u + 2), i + 1)
                        if MOD_FFN[l]:
                            mod(i * k + (u + 3), i + m)
                        hidden_high(i)
                    ahead(split, u + (n - 1) * k + 1)
                    if MOD_FFN[l]:
                        mod(u + n * k - 1, m + n - 1)
                    hidden_high(n - 1)
                    if g == 1:
                        gates(l, 1)
                    u, _, use2 = plan.at[(l, "down", g)]
                    for i in range(ND):
                        if n == 4:
                            ahead(split, u + i)
                            act.wait_ge(w_used, (u + i + 1) * UNIT)
                        else:
                            ahead(split, u, 2 * n * i, 2 * n)
                            act.wait_ge(w_used, u * UNIT + 2 * n * (i + 1))
                        for s in range(2):
                            b = f"{'AB'[i % 2]}{s}"
                            if g == 0:
                                act.copy(f[:, s, i * CH:(i + 1) * CH], bank[b][:]).then_inc(freed[b], 1)
                            elif g == 2:
                                act.wait_ge(freed[b], use2[b] + i // 2 + 2)
                                square(f[:, s, i * CH:(i + 1) * CH], ssq[:, s, i:i + 1])
                if l + 1 < DEPTH:
                    u, m, _ = plan.at[(l, "mod_pre_mix")]
                    for i in range(MOD_PRE_MIX):
                        mod(u + i, m + i)

        @block.vector
        def _(dve):
            own = [0]
            n_hi = [0]

            def link(ins):
                own[0] += 1
                ins.then_inc(dve_own, 1)
                dve.wait_ge(dve_own, own[0])

            def split(u, ph):
                if past_end(u, ph):
                    return
                dve.wait_ge(hi_ready, u * UNIT + (ph + 1))
                if not (isinstance(u, int) and u * UNIT + ph < RING):
                    dve.wait_ge(w_used, u * UNIT + (ph - RING + 1))
                dve.tensor_tensor(wlo[:, ph % RING], raw[:, ph % RING], whi[:, ph % RING].bitcast(F32),
                                  ALU.subtract).then_inc(lo_ready, 1)

            def fill_of(b, i):
                dve.wait_ge(filled[b], plan.fill.get((b, i), i + 1) if isinstance(i, int) else i + 1)

            def mod(u, i):
                ahead(split, u)
                mod_cols(i)

            def mod_cols(i):
                dve.wait_ge(filled["T"], i + 1)
                dve.tensor_scalar(modt[:, bass.ds(i * 8, 8)], bank["T"][:, 0:8], 1.0, None, ALU.mult).then_inc(freed["T"], 1)

            def mean_square(sums, j):
                dve.wait_ge(sq_ready, 8 * j)
                link(dve.tensor_reduce(msum[:], sums, AX_X, ALU.add))
                dve.tensor_scalar(ms[:], msum[:], 1.0 / D, EPS, ALU.mult, ALU.add).then_inc(ms_ready, 1)
                dve.wait_ge(rstd_ready, j)

            def low(dst, src, hi, s_out):
                n_hi[0] += 1
                dve.wait_ge(hi_x, n_hi[0])
                dve.tensor_tensor(dst, src, hi.bitcast(F32), ALU.subtract).then_inc(s_out, 1)

            def pre(l, which):
                v = 3 * which
                dve.wait_ge(freed["T"], mod_done(l, v + 1) + 1)
                link(dve.tensor_tensor(scal[:], mod_t(l, v + 1), mod_b(l, v + 1), ALU.add))
                dve.tensor_tensor(shift[:], mod_t(l, v), mod_b(l, v), ALU.add)
                dve.scalar_tensor_tensor(out=scal[:], in0=scal[:], scalar=1.0, in1=vec(2 * which, l),
                                         op0=ALU.add, op1=ALU.mult).then_inc(vec_ready, 1)
                mean_square(ssx[:], 4 * l + 2 * which + 1)
                for s in range(2):
                    dve.tensor_scalar(f[:, s, :], x[:, s, :], rstd[:, s:s + 1], None, ALU.mult).then_inc(xn_ready, 1)
                dve.wait_ge(vec_ready, 2 * l + which + 1)
                for b, uses in enumerate(plan.at[(l, "pre_uses", which)]):
                    bk, i = uses[0]
                    fill_of(bk, i)
                    if b:
                        dve.wait_ge(xt_ready, xt_count(l, which) - 8 + 2 * b)
                    for t in range(4):
                        k = 4 * b + t
                        ins = dve.tensor_scalar(xtmp[:, 0, t, :], bank[bk][:, t * P:(t + 1) * P], scal[:, k, 0:1],
                                                shift[:, k, 0:1], ALU.mult, ALU.add)
                    ins.then_inc(freed[bk], 1)
                    for s in range(2):
                        t = (slice(None), slice(4 * b, 4 * b + 4), slice(s * P, (s + 1) * P))
                        low(xt_lo[t], xtmp[:, s], xt_hi[t], xt_ready)

            def gate_vector(l, which):
                v = 3 * which + 2
                dve.wait_ge(freed["T"], mod_done(l, v) + 1)
                link(dve.tensor_tensor(gatev[:], mod_t(l, v), mod_b(l, v), ALU.add))
                dve.tensor_tensor(gatev[:], gatev[:], vec(2 * which + 1, l), ALU.mult).then_inc(gate_ready, 1)

            def gates(l, which):
                if which == 0:
                    dve.wait_ge(kv_stored, 16 * 4 * (l + 1))
                for n, uses in enumerate(plan.at[(l, "gate_uses", which)]):
                    bk, i = uses[1]
                    fill_of(bk, i)
                    dve.tensor_copy(gate[:, 1, n * CH:(n + 1) * CH], bank[bk][:]).then_inc(freed[bk], 1)

            def post(l, which):
                mean_square(ssq[:], 4 * l + 2 * which + 2)
                uses = plan.at[(l, "gate_uses", which)][-1]
                for bk, i in uses:
                    dve.wait_ge(freed[bk], i + 2)
                for n in range(ND):
                    c = slice(n * CH, (n + 1) * CH)
                    for s in range(2):
                        ins = dve.scalar_tensor_tensor(out=f[:, s, c], in0=f[:, s, c], scalar=rstd[:, s:s + 1],
                                                       in1=gate[:, s, c], op0=ALU.mult, op1=ALU.mult)
                    link(ins)
                    for s in range(2):
                        dve.tensor_tensor(x[:, s, c], x[:, s, c], f[:, s, c], ALU.add).then_inc(x_new, 1)

            def attention(l):
                dve.wait_ge(att_loaded, 16 * N_ATT * (l + 1))
                dve.tensor_tensor(bias[:], bias[:], edge[:].unsqueeze(1).broadcast_to([P, NH, P]), ALU.add)
                link(dve.tensor_scalar(nsink[:], sink[:], -1.0, None, ALU.mult))
                for step, banks, (u, m) in plan.at[(l, "attention")]:
                    kind = step[0]
                    if kind == "mod":
                        mod(u, m)
                    elif kind in ("turn", "turn_ck", "turn_ws"):
                        b, i = banks[0]
                        dst = {"turn": qkt, "turn_ck": ckt, "turn_ws": wst}[kind]
                        j = step[-1] if kind != "turn_ws" else 0
                        if b == "X1":
                            fill_of(b, i)
                            dve.tensor_copy(dst[:, 4 * j:4 * j + 4, :], four(bank[b][:])).then_inc(freed[b], 1)
                    elif kind == "score":
                        n = step[1]
                        s, ty = divmod(n, 2)
                        w = P * (1 + s)
                        for (b, i), heads in zip(banks, score_banks(n)):
                            fill_of(b, i)
                            k = len(heads)
                            sc = bank[b][:, 0:k * w].rearrange("p (h w) -> p h w", w=w)
                            hs = slice(heads[0], heads[0] + k)
                            if n == 2:
                                dve.scalar_tensor_tensor(out=prob[:, 0, hs, 0:P], in0=sc[:, :, 0:P], scalar=SCALE,
                                                         in1=bias[:, hs, :], op0=ALU.mult, op1=ALU.add)
                                ins = dve.tensor_scalar(prob[:, 0, hs, P:w], sc[:, :, P:w], SCALE, None, ALU.mult)
                                ins.then_inc(freed[b], 1)
                            else:
                                ins = dve.tensor_reduce(rmax[:, n, hs], sc, AX_X, ALU.max)
                        if n == 2:
                            dve.wait_ge(freed[b], i + 2)
                            ins = dve.tensor_reduce(rmax[:, n, :], prob[:, 0, :, :], AX_X, ALU.max)
                        link(ins)
                        if ty:
                            link(dve.scalar_tensor_tensor(out=nmax[:, n, :], in0=rmax[:, n, :], scalar=-SCALE,
                                                          in1=nsink[:], op0=ALU.mult, op1=ALU.min))
                            dve.tensor_tensor(esink[:, n, :], nmax[:, n, :], sink[:], ALU.add).then_inc(nm_ready, 1)
                        else:
                            dve.tensor_scalar(nmax[:, n, :], rmax[:, n, :], -1.0 if n == 2 else -SCALE, None,
                                              ALU.mult).then_inc(nm_ready, 1)
                    elif kind == "soft":
                        n = step[1]
                        s, ty = divmod(n, 2)
                        w = P * (1 + s)
                        dve.wait_ge(exp_ready, 4 * l + n + 1)
                        if ty:
                            link(dve.tensor_tensor(den[:, n, :], den[:, n, :], esink[:, n, :], ALU.add))
                        link(dve.reciprocal(den[:, n, :], den[:, n, :]))
                        pr = prob[:, n % 2, :, 0:w]
                        dve.tensor_tensor(pr, pr, den[:, n, :].unsqueeze(2).broadcast_to([P, NH, w]),
                                          ALU.mult).then_inc(pn_ready, 1)
                    elif kind == "value":
                        n = step[1]
                        s, ty = divmod(n, 2)
                        for j, (b, i) in enumerate(banks[:-2]):
                            if b == "X1":
                                fill_of(b, i)
                                k = min(4, NH * (1 + s) - 4 * j)
                                dve.tensor_copy(pt[:, 4 * j:4 * j + k, :], four(bank[b][:])[:, 0:k, :]).then_inc(freed[b], 1)
                        for (b, i), heads in zip(banks[-2:], (range(0, 4), range(4, 6))):
                            k = len(heads)
                            k0 = ty * NH + heads[0]
                            t = (slice(None), slice(k0, k0 + k), slice(s * P, (s + 1) * P))
                            low(xt_lo[t], four(bank[b][:])[:, 0:k, :], xt_hi[t], freed[b])
                    elif kind == "norm_v":
                        s = step[1]
                        v = z[:, s, V_C:W_IN]
                        dve.wait_ge(gelu_ready, 2 * l + s + 1)
                        link(dve.bn_stats(vstat[:, s, :], v))
                        link(dve.bn_aggr(vmv[:, s, :], vstat[:, s, :]))
                        dve.tensor_scalar(vmv[:, s, 1:2], vmv[:, s, 1:2], EPS, None, ALU.add).then_inc(vmv_ready, 1)
                        dve.wait_ge(vrstd_ready, 2 * l + s + 1)
                        link(dve.tensor_scalar(v, v, vmv[:, s, 0:1], vrstd[:, s:s + 1], ALU.subtract, ALU.mult))
                        link(dve.tensor_tensor(v, v, ln_g[:], ALU.mult))
                        dve.tensor_tensor(v, v, ln_b[:], ALU.add).then_inc(vn_ready, 1)
                    elif kind == "gate_c":
                        s = step[1]
                        b, i = banks[0]
                        fill_of(b, i)
                        for g in range(GC):
                            ug = z[:, s, U_C + g * P:U_C + (g + 1) * P]
                            c = 3 * P + 2 * KD + l * GC + g
                            ins = dve.scalar_tensor_tensor(out=ug, in0=bank[b][:, g * P:(g + 1) * P],
                                                           scalar=vcols[:, c:c + 1], in1=ug, op0=ALU.add, op1=ALU.mult)
                        ins.then_inc(freed[b], 1)
                    elif kind == "turn_c":
                        s = step[1]
                        b, i = banks[0]
                        t = (slice(None), slice(12, 16), slice(s * P, (s + 1) * P))
                        low(xt_lo[t], four(bank[b][:]), xt_hi[t], freed[b])

            dve.memset(vrows[:], 0.0).then_inc(vrows_clear, 1)
            dve.memset(minus_half[:], -0.5)
            dve.memset(cond[:].bitcast(F32), 0.0)
            for b in BANKS:
                dve.memset(clear[:, BANKS.index(b):BANKS.index(b) + 1], 0.0).then_inc(freed[b], 1)
            fill_of("X0", 0)
            dve.tensor_copy(vcols[:], bank["X0"][:]).then_inc(freed["X0"], 1)
            dve.wait_ge(silu_ready, 1)
            ct = cond[:, 0:4 * KD].rearrange("p (t j) -> p t j", j=4)
            sc = silu_c[:].rearrange("p c t -> p t c")
            link(dve.tensor_copy(ct[:, :, 0:2], sc))
            dve.tensor_tensor(ct[:, :, 2:4], sc, ct[:, :, 0:2].bitcast(F32), ALU.subtract).then_inc(cond_ready, 1)
            for j in range(LEAD):
                split(0, j)
            u, m, _ = plan.at[("init",)]
            with dve.Fori(0, MOD_INIT) as i:
                mod(i + u, i + m)
            for l in range(DEPTH):
                pre(l, 0)
                u, m, use = plan.at[(l, "win")]
                with dve.Fori(0, W_INC) as i:
                    ahead(split, i * 2 + u)
                    ahead(split, i * 2 + (u + 1))
                    dve.wait_ge(w_used, i * (2 * UNIT) + (u + 2) * UNIT)
                    for s in range(2):
                        dve.tensor_scalar(z[:, s, bass.ds(i * CH, CH)], bank[f"A{s}"][:], 1.0, None,
                                          ALU.mult).then_inc(freed[f"A{s}"], 1)
                    mod_cols(i + m)
                gate_vector(l, 0)
                attention(l)
                gates(l, 0)
                u, _, use = plan.at[(l, "out")]
                for i in range(ND):
                    ahead(split, u + i)
                post(l, 0)
                u, m, _ = plan.at[(l, "mod_pre_ffn")]
                for i in range(MOD_PRE_FFN[l]):
                    mod(u + i, m + i)
                pre(l, 1)
                for g, (c0, n) in enumerate(GROUPS):
                    u, m, use = plan.at[(l, "up", g)]
                    k = 3 if MOD_FFN[l] else 2

                    def multiply(u, i):
                        dve.wait_ge(w_used, u * UNIT + UNIT)
                        dve.wait_ge(filled["X1"], i + use["X1"])
                        for s in range(2):
                            dve.wait_ge(freed[f"A{s}"], i + (use[f"A{s}"] + 2))
                            dve.tensor_tensor(hid[:, s, :], sil[:, s, :], bank[f"B{s}"][:],
                                              ALU.mult).then_inc(freed[f"B{s}"], 1)

                    def hidden_low(i, first):
                        for s in range(2):
                            dve.wait_ge(ht_hi_ready, i * 2 + (first + s + 1))
                            t = (slice(None), bass.ds(i * 4, 4), slice(s * P, (s + 1) * P))
                            dve.tensor_tensor(ht_lo[t], four(bank[f"X{s}"][:]), ht_hi[t].bitcast(F32),
                                              ALU.subtract).then_inc(freed[f"X{s}"], 1)

                    first = 2 * (FFC * l + c0)
                    ahead(split, u)
                    with dve.Fori(0, n - 1) as i:
                        ahead(split, i * k + (u + 1))
                        multiply(i * k + (u + 1), i)
                        ahead(split, i * k + (u + 2))
                        if MOD_FFN[l]:
                            ahead(split, i * k + (u + 3))
                        hidden_low(i, first)
                        if MOD_FFN[l]:
                            mod_cols(i + m)
                    ahead(split, u + (n - 1) * k + 1)
                    multiply(u + (n - 1) * k + 1, n - 1)
                    if MOD_FFN[l]:
                        ahead(split, u + n * k - 1)
                    hidden_low(n - 1, first)
                    if MOD_FFN[l]:
                        mod_cols(m + n - 1)
                    if g == 0:
                        gate_vector(l, 1)
                    if g == 1:
                        gates(l, 1)
                    u, _, use2 = plan.at[(l, "down", g)]
                    for i in range(ND):
                        if n == 4:
                            ahead(split, u + i)
                            dve.wait_ge(w_used, (u + i + 1) * UNIT)
                        else:
                            ahead(split, u, 2 * n * i, 2 * n)
                            dve.wait_ge(w_used, u * UNIT + 2 * n * (i + 1))
                        for s in range(2):
                            b = f"{'AB'[i % 2]}{s}"
                            if g:
                                c = slice(i * CH, (i + 1) * CH)
                                dve.tensor_tensor(f[:, s, c], f[:, s, c], bank[b][:], ALU.add).then_inc(freed[b], 1)
                post(l, 1)
                if l + 1 < DEPTH:
                    u, m, _ = plan.at[(l, "mod_pre_mix")]
                    for i in range(MOD_PRE_MIX):
                        mod(u + i, m + i)


_INS = ['x_prompt', 'x_sample', 'cache_a_k', 'cache_a_v', 'cache_b_k', 'cache_b_v', 'c', 'c_ctx', 'mod_w', 'mod_b',
        'norm_mix_pre', 'norm_mix_post', 'norm_ffn_pre', 'norm_ffn_post', 'w_in', 'w_out', 'rpb_a', 'sink_b',
        'gmlp_ln_g', 'gmlp_ln_b', 'gmlp_w', 'gmlp_b', 'w_gate', 'w_up', 'w_down']
_OUTS = [(1, 128, 2048), (1, 128, 2048), (1, 2, 6, 128, 128), (1, 2, 6, 128, 128), (1, 2, 2, 128, 128), (1, 2, 2, 128, 128)]


def constants():
    t = np.arange(P)
    half = 32
    freqs = (np.float32(10000.0) ** (-np.arange(half, dtype=np.float32) / np.float32(half))).astype(np.float32)
    rope = np.zeros((P, 2, 2, 2, half), np.float32)
    for axis, pos in enumerate((t // GRID, t % GRID)):
        ang = pos.astype(np.float32)[:, None] * freqs[None, :]
        rope[:, 0, axis, 0] = rope[:, 0, axis, 1] = np.cos(ang)
        rope[:, 1, axis, 0] = -np.sin(ang)
        rope[:, 1, axis, 1] = np.sin(ang)
    col = t % GRID
    c0 = np.clip(col - 8, 0, GRID - 16)
    ok = (col[None, :] >= c0[:, None]) & (col[None, :] < c0[:, None] + 16)
    rsel = np.zeros((4, 2), np.float32)
    rsel[[0, 2], 0] = rsel[[1, 3], 1] = 1
    return {
        "c_ident": np.eye(P, dtype=np.float32), "c_rsel": rsel, "c_rope": rope.reshape(P, 2 * P),
        "c_edge": np.where(ok, 0, NEG).astype(np.float32),
        "c_zero": np.zeros((DEPTH * NH * 3, 2 * GRID - 1), np.float32),
    }


def kernel(**inputs):
    import concourse.bacc as bacc
    from concourse.bass_utils import run_bass_kernel_spmd

    nc = bacc.Bacc("TRN2", target_bir_lowering=False, num_devices=1)
    arrays, args = {}, {}
    for name, v in [(n, inputs[n]) for n in _INS] + list(constants().items()):
        v = np.ascontiguousarray(v)
        arrays[f"in_{name}"] = v
        args[name] = nc.dram_tensor(f"in_{name}", v.shape, F32, kind="ExternalInput").ap()
    for i, shape in enumerate(_OUTS):
        args[f"out_{i}"] = nc.dram_tensor(f"out_{i}", shape, F32, kind="ExternalOutput").ap()
    build_program(nc, args)
    r = run_bass_kernel_spmd(nc, [arrays], core_ids=[0])
    return tuple(r.results[0][f"out_{i}"] for i in range(len(_OUTS)))
```

```python
from contextlib import ExitStack

import numpy as np

import concourse.bass as bass
from concourse import mybir

F32 = mybir.dt.float32
F32R = mybir.dt.float32r
ALU = mybir.AluOpType
ACT = mybir.ActivationFunctionType
AX_X = mybir.AxisListType.X

P = 128
D = 2048
KD = D // P
DEPTH = 2
CH = 512
ND = D // CH
NH = 6
KVB = 2
GC = 4
W_IN = 4608
W_INC = W_IN // CH
Q_A, K_A, V_A, Q_B, K_B, V_B, U_C, V_C = 0, 768, 1536, 2304, 3072, 3328, 3584, 4096
FF = 5632
FFC = FF // CH
GROUPS = [(0, 4), (4, 4), (8, 3)]
NMODC = 6 * D // CH
SCALE = float(P) ** -0.5
EPS = 1e-6
NEG = -1e30
GRID = 64

KB = 2
UNIT = KD // KB
RING = 4
LEAD = 4
IN_ONE = {1: range(0, 4), 5: range(4, 8)}
IN_FIRST, IN_SECOND = {3: range(0, 4)}, {3: range(4, 8)}
LOAD_ONE = {0: [0], 1: [1], 2: [2], 3: [3], 4: [4], 5: [5], 6: [6], 7: [7]}
LOAD_FIRST, LOAD_SECOND = ({0: [j], 2: [j + 1], 4: [j + 2], 6: [j + 3]} for j in (0, 4))

MOD_INIT = 8
MOD_WIN = W_INC // 2
MOD_ATT = 6
MOD_OUT = ND // 2


def mod_up(l, g):
    return g == 0 or l + 1 < DEPTH

BANKS = ["A0", "A1", "B0", "B1", "M", "X0", "X1", "T"]

def attention_steps():
    def mods(*parts):
        return [(f"mod_{p}",) for p in parts]
    s = [("turn", 0, b) for b in range(5)] + mods("first") + [("score", 0), ("turn_ws",), ("turn_ck", 0), ("turn_ck", 1)]
    s += mods("second") + [("score", 1), ("soft", 0)] + [("turn", 1, b) for b in range(3)] + mods("tail", "first")
    s += [("norm_v", 0), ("turn", 1, 3), ("turn", 1, 4), ("value", 0), ("soft", 1), ("score", 2)] + mods("second")
    s += [("norm_v", 1), ("value", 1)] + mods("tail", "first") + [("score", 3), ("gate_c", 0), ("gate_c", 1)]
    s += mods("second") + [("soft", 2)] + mods("tail", "first") + [("value", 2)] + mods("second")
    s += [("turn_c", 0), ("turn_c", 1), ("soft", 3)] + mods("tail", "first", "second") 
    s += [("value", 3)] + mods("tail", "first", "second", "tail")
    return s


def score_banks(n):
    return [range(0, 4), range(4, 6)] if n < 2 else [range(0, 2), range(2, 4), range(4, 6)]


class Plan:

    def __init__(self):
        self.unit, self.mod, self.use = 0, 0, dict.fromkeys(BANKS, 0)
        self.fills, self.fill = dict.fromkeys(BANKS, 0), {}
        self.at = {}
        self.turn_bank = 0
        self.acc_bank = 0

        self.mark(("init",))
        self.take("X0")
        self.mods(MOD_INIT)
        for l in range(DEPTH):
            self.pre(l, 0)
            self.mark((l, "win"))
            self.unit += W_INC
            self.mods(MOD_WIN)
            self.takes(["A0", "A1"], (W_INC + 1) // 2)
            self.takes(["B0", "B1"], W_INC // 2)
            self.mark((l, "att"))
            self.attention(l)
            self.gate(l, 0)
            self.mark((l, "out"))
            self.unit += ND
            self.takes(["A0", "A1", "B0", "B1"], ND // 2)
            self.mods(MOD_OUT)
            self.pre(l, 1)
            for g, (_, n) in enumerate(GROUPS):
                self.mark((l, "up", g))
                self.unit += 2 * n
                self.takes(["A0", "A1", "B0", "B1", "X0", "X1"], n)
                if mod_up(l, g):
                    self.mods(n)
                if g == 1:
                    self.gate(l, 1)
                self.mark((l, "down", g))
                self.unit += n if n < 4 else ND
                if g == len(GROUPS) - 1 and l + 1 < DEPTH:
                    self.mods(1)
                self.takes(["A0", "A1", "B0", "B1"], ND // 2)

    def mark(self, key):
        self.at[key] = (self.unit, self.mod, dict(self.use))

    def mods(self, n):
        self.mod += n
        self.takes(["M", "T"], n)

    def takes(self, banks, n):
        for b in banks:
            self.use[b] += n
            if b in ("X0", "X1", "T"):
                self.fills[b] += n

    def take(self, bank):
        self.use[bank] += 1
        self.fills[bank] += 1
        self.fill[(bank, self.use[bank] - 1)] = self.fills[bank]
        return bank, self.use[bank] - 1

    def turn(self):
        self.turn_bank ^= 1
        return self.take(("X0", "X1")[self.turn_bank])

    def acc(self):
        self.acc_bank = (self.acc_bank + 1) % 4
        return self.take(BANKS[self.acc_bank])

    def pre(self, l, which):
        self.mark((l, "pre", which))
        self.at[(l, "pre_uses", which)] = [[self.take(f"X{s}") for s in range(2)] for _ in range(KD // 4)]

    def gate(self, l, which):
        self.at[(l, "gate_uses", which)] = [[self.take(f"X{s}") for s in range(2)] for _ in range(ND)]

    def attention(self, l):
        uses = []
        for step in attention_steps():
            mine = self.mod
            banks = []
            if step[0] in ("turn", "turn_ck", "turn_ws", "turn_c"):
                banks = [self.turn()]
            elif step[0] == "score":
                banks = [self.acc() for _ in score_banks(step[1])]
            elif step[0] == "value":
                banks = [self.turn() for _ in range(2 if step[1] < 2 else 3)] + [self.acc() for _ in range(2)]
            elif step[0] == "gate_c":
                banks = [self.acc()]
            elif step[0] == "mod_first":
                self.mods(1)
            uses.append((step, banks, mine if step[0] == "mod_first" else mine - 1))
        self.at[(l, "attention")] = uses


def build_program(nc, a):
    plan = Plan()
    TOTAL = plan.unit * UNIT
    xin = [a["x_prompt"][0], a["x_sample"][0]]
    xout = [a["out_0"][0], a["out_1"][0]]

    def four(ap):
        return ap.rearrange("p (t c) -> p t c", t=4)

    with ExitStack() as ctx:
        def sem(name):
            return ctx.enter_context(nc.semaphore(name))

        def sb(name, shape, dt=F32, at=ctx):
            return at.enter_context(nc.sbuf_tensor(name, shape, dt))

        bank = {b: ctx.enter_context(nc.psum_tensor(f"bank_{b}", [P, CH], F32)) for b in BANKS}

        raw = sb("raw", [P, RING, KB, CH])
        mraw = sb("mraw", [P, RING, KB, CH])
        whi = sb("whi", [P, RING, KB, CH], F32R)
        wlo = sb("wlo", [P, RING, KB, CH], F32R)
        x = sb("x", [P, 2, D])
        xt_hi = sb("xt_hi", [P, KD, 2 * P], F32R)
        xt_lo = sb("xt_lo", [P, KD, 2 * P], F32R)
        ident = sb("ident", [P, P])
        rsel = sb("rsel", [P, 2])
        rope = sb("rope", [P, 2, P])
        edge = sb("edge", [P, P])
        vcols = sb("vcols", [P, 4 * P])
        silu_c = sb("silu_c", [P, 2, KD])
        cond = sb("cond", [P, KD * 2 + 32])
        mrow = sb("mrow", [P, CH])
        modt = sb("modt", [P, DEPTH * NMODC * 8])
        shift = sb("shift", [P, KD, 2])
        scal = sb("scal", [P, KD, 2])
        gatev = sb("gatev", [P, KD, 2])
        ssq = sb("ssq", [P, 2, ND])
        ssx = sb("ssx", [P, 2, ND])
        ms = sb("ms", [P, 2])
        rstd = sb("rstd", [P, 2])
        minus_half = sb("minus_half", [P, 2])
        junk = sb("junk", [P, CH])

        ffn = ExitStack()
        gate = sb("gate", [P, 2, D], F32, ffn)
        ht_hi = sb("ht_hi", [P, KD, 2 * P], F32R, ffn)
        ht_lo = sb("ht_lo", [P, KD, 2 * P], F32R, ffn)
        f = sb("f", [P, 2, D], F32, ffn)
        hid = sb("hid", [P, 2, CH], F32, ffn)
        sil = sb("sil", [P, 2, CH], F32, ffn)
        xtmp = sb("xtmp", [P, 2, 2, 4, P], F32, ffn)
        ffn.close()
        z = sb("z", [P, 2, W_IN])
        qkt = sb("qkt", [P, 20, P])
        cv = sb("cv", [P, NH + KVB, P])
        ckt = sb("ckt", [P, NH + KVB, P])
        bias = sb("bias", [P, NH, P])
        turned_b = sb("turned_b", [P, 8, P])
        prob = sb("prob", [P, 2, NH, 2 * P])
        pt = sb("pt", [P, 12, P])
        ln_g = sb("ln_g", [P, CH])
        vrows = four(z[:, 0, 0:4 * P])
        late = prob[:, 1].rearrange("p h c -> p (h c)").rearrange("p (t c) -> p t c", c=P)
        ck, ws = late[:, 0:8, :], late[:, 8:12, :]
        crossed, ln_b = pt[:, 0:8, :], pt[:, 8:12, :].rearrange("p t c -> p (t c)")
        wst = sb("wst", [P, GC, P])
        sink = sb("sink", [P, NH])
        nsink = sb("nsink", [P, NH])
        msum = sb("msum", [P, 2])
        clear = sb("clear", [P, len(BANKS)])
        rmax = sb("rmax", [P, 4, NH])
        nmax = sb("nmax", [P, 4, NH])
        den = sb("den", [P, 4, NH])
        esink = sb("esink", [P, 4, NH])
        vstat = sb("vstat", [P, 2, 6])
        vmv = sb("vmv", [P, 2, 2])
        vrstd = sb("vrstd", [P, 2])

        PADW = 2 * GRID - 1
        rpb_pad = nc.dram_tensor("rpb_pad", [DEPTH * NH * 3, PADW], F32, kind="Internal").ap()
        rpb_rows = nc.dram_tensor("rpb_rows", [GRID, DEPTH * NH * 3, PADW], F32, kind="Internal").ap()

        filled = {b: sem(f"filled_{b}") for b in BANKS}
        freed = {b: sem(f"freed_{b}") for b in BANKS}
        raw_landed = [sem(f"raw_landed_{i}") for i in range(RING)]
        mraw_landed = [sem(f"mraw_landed_{i}") for i in range(RING)]
        mod_used = sem("mod_used")
        hi_ready = sem("hi_ready")
        lo_ready = sem("lo_ready")
        w_used = sem("w_used")
        const_loaded = sem("const_loaded")
        x_loaded = sem("x_loaded")
        pad_cleared = sem("pad_cleared")
        pad_filled = sem("pad_filled")
        pad_copied = sem("pad_copied")
        att_loaded = sem("att_loaded")
        vrows_clear = sem("vrows_clear")
        silu_ready = sem("silu_ready")
        cond_ready = sem("cond_ready")
        dve_own = sem("dve_own")
        act_own = sem("act_own")
        pool_own = sem("pool_own")
        mrow_ready = sem("mrow_ready")
        xt_ready = sem("xt_ready")
        vec_ready = sem("vec_ready")
        sq_ready = sem("sq_ready")
        ms_ready = sem("ms_ready")
        rstd_ready = sem("rstd_ready")
        xn_ready = sem("xn_ready")
        gate_ready = sem("gate_ready")
        hi_x = sem("hi_x")
        x_new = sem("x_new")
        ht_hi_ready = sem("ht_hi_ready")
        gelu_ready = sem("gelu_ready")
        rope_ready = sem("rope_ready")
        nm_ready = sem("nm_ready")
        exp_ready = sem("exp_ready")
        pn_ready = sem("pn_ready")
        vmv_ready = sem("vmv_ready")
        vrstd_ready = sem("vrstd_ready")
        vn_ready = sem("vn_ready")
        kv_stored = sem("kv_stored")
        x_stored = sem("x_stored")

        def vec(v, l):
            c = (v * DEPTH + l) * KD
            return vcols[:, c:c + KD].unsqueeze(2).broadcast_to([P, KD, 2])

        def mod_b(l, v):
            c = P * (1 + l) + v * KD
            return vcols[:, c:c + KD].unsqueeze(2).broadcast_to([P, KD, 2])

        def mod_t(l, v):
            c = (l * 6 + v) * KD * 2
            return modt[:, c:c + KD * 2].rearrange("p (t c) -> p t c", c=2)

        def mod_done(l, v):
            return l * NMODC + (v + 1) * ND

        def xt_count(l, which):
            return 16 * l + 8 * (which + 1)

        def z_complete(engine, l):
            for b in ("A0", "A1", "B0", "B1"):
                engine.wait_ge(freed[b], plan.at[(l, "att")][2][b] + 1)

        N_CONST = 13
        N_ATT = 12

        block = ctx.enter_context(nc.Block())

        @block.sync
        def _(sp):
            def piece(u, ph, src):
                if not (isinstance(u, int) and u * UNIT + ph < RING):
                    sp.wait_ge(lo_ready, u * UNIT + (ph - RING + 1))
                sp.dma_start(raw[:, ph % RING], src.rearrange("(t p) n -> p t n", p=P)).then_inc(
                    raw_landed[ph % RING], 16)

            def chunk(u, w, row0, col, pieces=UNIT, ph=0):
                for j in range(pieces):
                    piece(u, ph + j, w[row0 + j * KB * P:row0 + (j + 1) * KB * P, bass.ds(col, CH)])

            def mod_chunk(m, l, js=range(UNIT)):
                for j in js:
                    if not (isinstance(m, int) and m * UNIT + j < RING):
                        sp.wait_ge(mod_used, m * UNIT + (j - RING + 1))
                    src = a["mod_w"][l, j * KB * P:(j + 1) * KB * P, bass.ds((m - l * NMODC) * CH, CH)]
                    sp.dma_start(mraw[:, j % RING], src.rearrange("(t p) n -> p t n", p=P)).then_inc(
                        mraw_landed[j % RING], 16)

            def both(u, w, col, m=0, l=0, behind={}, js=range(UNIT)):
                for j in js:
                    piece(u, j, w[j * KB * P:(j + 1) * KB * P, bass.ds(col, CH)])
                    if j in behind:
                        mod_chunk(m, l, behind[j])

            def first_unit(u, w, col):
                both(u, w, col, js=range(LEAD))

            def both_rest(u, w, col, m, l):
                for j in range(LEAD):
                    mod_chunk(m, l, LOAD_FIRST.get(j, []))
                both(u, w, col, m, l, LOAD_FIRST, range(LEAD, UNIT))

            _, m, _ = plan.at[("init",)]
            mod_chunk(m, 0, range(RING))
            first_unit(plan.at[(0, "win")][0], a["w_in"][0], 0)
            mod_chunk(m, 0, range(RING, UNIT))
            with sp.Fori(1, MOD_INIT) as i:
                mod_chunk(i + m, 0)
            for l in range(DEPTH):
                u, m, _ = plan.at[(l, "win")]
                w = a["w_in"][l]
                both_rest(u, w, 0, m, l)
                both(u + 1, w, CH, m, l, LOAD_SECOND)
                with sp.Fori(1, W_INC // 2) as i:
                    both(i * 2 + u, w, i * 2 * CH, i + m, l, LOAD_FIRST)
                    both(i * 2 + (u + 1), w, i * 2 * CH + CH, i + m, l, LOAD_SECOND)
                both(u + W_INC - 1, w, (W_INC - 1) * CH)
                u, m, _ = plan.at[(l, "out")]
                w = a["w_out"][l]
                first_unit(u, w, 0)
                for step, _, m_att in plan.at[(l, "attention")]:
                    if step[0] == "mod_first":
                        mod_chunk(m_att, l)
                both_rest(u, w, 0, m, l)
                both(u + 1, w, CH, m, l, LOAD_SECOND)
                with sp.Fori(1, ND // 2) as i:
                    both(i * 2 + u, w, i * 2 * CH, i + m, l, LOAD_FIRST)
                    both(i * 2 + (u + 1), w, i * 2 * CH + CH, i + m, l, LOAD_SECOND)
                first_unit(plan.at[(l, "up", 0)][0], a["w_gate"][l], 0)
                for g, (c0, n) in enumerate(GROUPS):
                    u, m, _ = plan.at[(l, "up", g)]
                    lm = l + (g > 0)
                    both(u, a["w_gate"][l], c0 * CH, js=range(0 if g else LEAD, UNIT))
                    with sp.Fori(0, n - 1) as i:
                        if mod_up(l, g):
                            both(i * 2 + (u + 1), a["w_up"][l], i * CH + c0 * CH, i + m, lm, LOAD_FIRST)
                            both(i * 2 + (u + 2), a["w_gate"][l], i * CH + (c0 + 1) * CH, i + m, lm, LOAD_SECOND)
                        else:
                            chunk(i * 2 + (u + 1), a["w_up"][l], 0, i * CH + c0 * CH)
                            chunk(i * 2 + (u + 2), a["w_gate"][l], 0, i * CH + (c0 + 1) * CH)
                    both(u + 2 * n - 1, a["w_up"][l], (c0 + n - 1) * CH, m + n - 1, lm, LOAD_ONE if mod_up(l, g) else {})
                    u, m, _ = plan.at[(l, "down", g)]
                    if n == 4:
                        with sp.Fori(0, ND) as i:
                            chunk(i + u, a["w_down"][l], c0 * CH, i * CH)
                    else:
                        for i in range(ND):
                            chunk(u, a["w_down"][l], c0 * CH, i * CH, 2 * n, 2 * n * i)
                            if i < 2 and l + 1 < DEPTH:
                                mod_chunk(m, l + 1, range(4 * i, 4 * i + 4))
                if l + 1 < DEPTH:
                    first_unit(plan.at[(l + 1, "win")][0], a["w_in"][l + 1], 0)
            sp.wait_ge(kv_stored, 16 * 4 * DEPTH)
            sp.wait_ge(x_stored, 32)

        @block.gpsimd
        def _(pool):
            own = [0]

            def link(ins):
                own[0] += 1
                ins.then_inc(pool_own, 1)
                pool.wait_ge(pool_own, own[0])

            def load(dst, src, s):
                pool.dma_start(dst, src).then_inc(s, 16)

            pool.wait_ge(vrows_clear, 1)
            for v, name in enumerate(["norm_mix_pre", "norm_mix_post", "norm_ffn_pre", "norm_ffn_post"]):
                load(vrows[v * 32:v * 32 + 32, 0, :], a[name].rearrange("l (t p) -> (l t) p", p=P), const_loaded)
            for l in range(DEPTH):
                load(vrows[0:96, 1 + l, :], a["mod_b"][l].rearrange("(t p) -> t p", p=P), const_loaded)
            load(vrows[0:16, 3, :], a["c_ctx"].rearrange("(t p) -> t p", p=P), const_loaded)
            load(vrows[16:32, 3, :], a["c"][0].rearrange("(t p) -> t p", p=P), const_loaded)
            load(vrows[32:40, 3, :], a["gmlp_b"].rearrange("l g p -> (l g) p"), const_loaded)
            load(ident[:], a["c_ident"], const_loaded)
            load(rsel[:], a["c_rsel"], const_loaded)
            load(rope[:], a["c_rope"].rearrange("p (a b) -> p a b", a=2), const_loaded)
            load(edge[:], a["c_edge"], const_loaded)
            for s in range(2):
                load(x[:, s, :], xin[s], x_loaded)
            load(rpb_pad, a["c_zero"], pad_cleared)
            pool.wait_ge(pad_cleared, 16)
            load(rpb_pad[:, GRID - 16:GRID + 15].rearrange("(g r) c -> g r c", r=3),
                 a["rpb_a"].rearrange("l h r c -> (l h) r c")[:, 6:9, :], pad_filled)
            pool.wait_ge(pad_filled, 16)
            load(rpb_rows, rpb_pad.unsqueeze(0).broadcast_to([GRID, DEPTH * NH * 3, PADW]), pad_copied)
            pool.wait_ge(pad_copied, 16)

            def power(src, dst, s_in, n_in, s_out):
                pool.wait_ge(s_in, n_in)
                pool.tensor_tensor(dst, src, minus_half[:, 0:dst.shape[-1]], ALU.pow).then_inc(s_out, 1)

            n_rstd = 0
            for l in range(DEPTH):
                n_rstd += 1
                power(ms[:], rstd[:], ms_ready, n_rstd, rstd_ready)
                pool.wait_ge(xt_ready, xt_count(l, 0))
                load(ck[:, 0:NH, :], a["cache_a_k"][0, l].rearrange("h k d -> k h d"), att_loaded)
                load(ck[:, NH:, :], a["cache_b_k"][0, l].rearrange("h k d -> k h d"), att_loaded)
                load(cv[:, 0:NH, :], a["cache_a_v"][0, l].rearrange("h k d -> k h d"), att_loaded)
                load(cv[:, NH:, :], a["cache_b_v"][0, l].rearrange("h k d -> k h d"), att_loaded)
                load(ln_g[:], a["gmlp_ln_g"][l:l + 1, :].broadcast_to([P, CH]), att_loaded)
                load(ln_b, a["gmlp_ln_b"][l:l + 1, :].broadcast_to([P, CH]), att_loaded)
                load(ws, a["gmlp_w"][l].rearrange("g p q -> p g q"), att_loaded)
                load(sink[:], a["sink_b"][l:l + 1].rearrange("l g r -> l (g r)").broadcast_to([P, NH]), att_loaded)
                for qr in range(2):
                    for kr in range(2):
                        first = (l * NH * 3 + kr - qr + 1) * PADW + GRID - 1
                        src = bass.AP(rpb_rows.tensor, first,
                                      [[DEPTH * NH * 3 * PADW - 1, GRID], [3 * PADW, NH], [1, GRID]])
                        load(bias[qr * GRID:(qr + 1) * GRID, :, kr * GRID:(kr + 1) * GRID], src, att_loaded)
                z_complete(pool, l)
                zb = z[:, 1, Q_B:V_B].rearrange("p (h c) -> p h c", c=P)
                z5 = z[:, 1, Q_B:V_B].rearrange("p (h i c) -> p h i c", i=2, c=32)
                c5 = crossed.rearrange("p h c -> p (h c)").rearrange("p (h i c) -> p h i c", i=2, c=32)
                sn = rope[:, 1, :].rearrange("p (j i c) -> p j i c", j=2, i=2)
                pool.wait_ge(const_loaded, 16 * N_CONST)
                pool.tensor_tensor(turned_b[:], zb, rope[:, 0:1, :].broadcast_to([P, 8, P]), ALU.mult).then_inc(pool_own, 1)
                for i in range(2):
                    for j in range(2):
                        ins = pool.tensor_tensor(c5[:, j::2, i, :], z5[:, j::2, 1 - i, :],
                                                 sn[:, j:j + 1, i, :].broadcast_to([P, 8, 32]), ALU.mult)
                        ins.then_inc(pool_own, 1)
                own[0] += 5
                pool.wait_ge(pool_own, own[0])
                pool.tensor_tensor(turned_b[:], turned_b[:], crossed, ALU.add).then_inc(rope_ready, 1)
                for dst, col, n in ((a["out_2"], K_A, NH), (a["out_3"], V_A, NH), (a["out_4"], K_B, KVB), (a["out_5"], V_B, KVB)):
                    pool.dma_start(dst[0, l].rearrange("h t d -> t h d"),
                                   z[:, 0, col:col + n * P].rearrange("p (h c) -> p h c", c=P)).then_inc(kv_stored, 16)
                for s in range(2):
                    power(vmv[:, s, 1:2], vrstd[:, s:s + 1], vmv_ready, 2 * l + s + 1, vrstd_ready)
                for _ in range(3):
                    n_rstd += 1
                    power(ms[:], rstd[:], ms_ready, n_rstd, rstd_ready)
            for s in range(2):
                pool.wait_ge(x_new, 16 * DEPTH)
                pool.dma_start(xout[s], x[:, s, :]).then_inc(x_stored, 16)

        @block.tensor
        def _(pe):
            def free(b, i):
                pe.wait_ge(freed[b], i + 1)

            def read(b, i):
                pe.wait_ge(freed[b], i + 2)

            def dense(u, pair, i, hi, lo, nk=KD, ph=0, ready=None, m=None, behind={}):
                free(pair + "0", i)
                free(pair + "1", i)
                for j in range(nk // KB):
                    pe.wait_ge(lo_ready, u * UNIT + (ph + j + 1))
                    slot = (ph + j) % RING
                    for kb in range(KB):
                        k = j * KB + kb
                        if ready:
                            ready(k)
                        for s in range(2):
                            t = slice(s * P, (s + 1) * P)
                            for n, (xs, ws_) in enumerate([(lo, whi), (hi, wlo), (hi, whi)]):
                                mm = pe.matmul(bank[f"{pair}{s}"][:], xs[:, k, t], ws_[:, slot, kb, :],
                                               start=(k == 0 and n == 0), stop=(k == nk - 1 and n == 2))
                    mm.then_inc(w_used, 1)
                    if j in behind:
                        mod(m, behind[j])

            def mod(m, js=range(UNIT)):
                for j in js:
                    pe.wait_ge(mraw_landed[j % RING], m * (16 * UNIT // RING) + 16 * (j // RING + 1))
                    for kb in range(KB):
                        k = j * KB + kb
                        g = 32 * (k % 4)
                        mm = pe.matmul(bank["M"][g:g + 32, :], cond[:, 2 * k:2 * k + 32], mraw[:, j % RING, kb, :],
                                       start=(k < 4), stop=(k >= KD - 4))
                    mm.then_inc(mod_used, 1)

            def mod_tail(i):
                pe.wait_ge(mrow_ready, i + 1)
                free("T", i)
                for t in range(4):
                    mm = pe.matmul(bank["T"][:, 2 * t:2 * t + 2], mrow[:, t * P:(t + 1) * P], rsel[:],
                                   start=True, stop=True)
                mm.then_inc(filled["T"], 1)

            def turn(b, i, tiles, skip_free=False):
                free(b, i)
                for n, t in enumerate(tiles):
                    mm = pe.transpose(bank[b][:, n * P:(n + 1) * P], t, ident[:])
                mm.then_inc(filled[b], 1)

            def pre(l, which):
                for b, uses in enumerate(plan.at[(l, "pre_uses", which)]):
                    for s, (bk, i) in enumerate(uses):
                        pe.wait_ge(xn_ready, 4 * l + 2 * which + s + 1)
                        turn(bk, i, [f[:, s, (4 * b + t) * P:(4 * b + t + 1) * P] for t in range(4)])

            def xt_ready_at(l, which):
                def ready(k):
                    if k % 4 == 0:
                        pe.wait_ge(xt_ready, xt_count(l, which) - 8 + 2 * (k // 4 + 1))
                return ready

            def gates(l, which):
                pe.wait_ge(gate_ready, 2 * l + which + 1)
                for n, uses in enumerate(plan.at[(l, "gate_uses", which)]):
                    for s, (bk, i) in enumerate(uses):
                        turn(bk, i, [gatev[:, 4 * n + t, s:s + 1].broadcast_to([P, P]) for t in range(4)])

            def attention(l):
                got = {}
                for step, banks, m in plan.at[(l, "attention")]:
                    kind = step[0]
                    if kind in ("mod_first", "mod_second"):
                        mod(m, range(UNIT // 2) if kind == "mod_first" else range(UNIT // 2, UNIT))
                    elif kind == "mod_tail":
                        mod_tail(m)
                    elif kind == "turn":
                        s, b = step[1:]
                        if s == 1 and b == 3:
                            pe.wait_ge(rope_ready, l + 1)
                        turn(*banks[0], [z[:, s, h * P:(h + 1) * P] if h < 12 else
                                         turned_b[:, h - 12, :] if s else z[:, 0, Q_B + (h - 12) * P:Q_B + (h - 11) * P]
                                         for h in range(4 * b, 4 * b + 4)])
                    elif kind == "turn_ck":
                        b = step[1]
                        pe.wait_ge(att_loaded, 16 * N_ATT * (l + 1))
                        turn(*banks[0], [ck[:, h, :] for h in range(4 * b, 4 * b + 4)])
                    elif kind == "turn_ws":
                        pe.wait_ge(att_loaded, 16 * N_ATT * (l + 1))
                        turn(*banks[0], [ws[:, g, :] for g in range(GC)])
                    elif kind == "score":
                        n = step[1]
                        s, ty = divmod(n, 2)
                        for b, i in [got[("turn", s, j)][0] for j in range(5)] + [got[("turn_ck", j)][0] for j in range(2 * s)]:
                            read(b, i)
                        for (b, i), heads in zip(banks, score_banks(n)):
                            free(b, i)
                            for j, h in enumerate(heads):
                                q, k, c = (h, 6 + h, h) if ty == 0 else (12 + h, 18 + h // 3, 6 + h // 3)
                                o = j * P * (1 + s)
                                mm = pe.matmul(bank[b][:, o:o + P], qkt[:, q, :], qkt[:, k, :], start=True, stop=True)
                                if s:
                                    mm = pe.matmul(bank[b][:, o + P:o + 2 * P], qkt[:, q, :], ckt[:, c, :],
                                                   start=True, stop=True)
                            mm.then_inc(filled[b], 1)
                    elif kind == "value":
                        n = step[1]
                        s, ty = divmod(n, 2)
                        pe.wait_ge(pn_ready, 4 * l + n + 1)
                        blocks = [prob[:, n % 2, h, w * P:(w + 1) * P] for h in range(NH) for w in range(1 + s)]
                        turns, outs = banks[:-2], banks[-2:]
                        for j, (b, i) in enumerate(turns):
                            turn(b, i, blocks[4 * j:4 * j + 4])
                        for b, i in turns:
                            read(b, i)
                        for (b, i), heads in zip(outs, (range(0, 4), range(4, 6))):
                            free(b, i)
                            for j, h in enumerate(heads):
                                kv = h if ty == 0 else 6 + h // 3
                                col = V_A + h * P if ty == 0 else V_B + (h // 3) * P
                                vs = [z[:, s, col:col + P]] + s * [cv[:, kv, :]]
                                for w, v in enumerate(vs):
                                    mm = pe.matmul(bank[b][:, j * P:(j + 1) * P], v, pt[:, h * (1 + s) + w, :],
                                                   start=(w == 0), stop=(w == s))
                            mm.then_inc(filled[b], 1)
                    elif kind == "gate_c":
                        s = step[1]
                        pe.wait_ge(vn_ready, 2 * l + s + 1)
                        read(*got[("turn_ws",)][0])
                        b, i = banks[0]
                        free(b, i)
                        for g in range(GC):
                            mm = pe.matmul(bank[b][:, g * P:(g + 1) * P], wst[:, g, :],
                                           z[:, s, V_C + g * P:V_C + (g + 1) * P], start=True, stop=True)
                        mm.then_inc(filled[b], 1)
                    elif kind == "turn_c":
                        s = step[1]
                        read(*got[("gate_c", s)][0])
                        turn(*banks[0], [z[:, s, U_C + g * P:U_C + (g + 1) * P] for g in range(GC)])
                    if banks:
                        got[step] = banks
                return got

            pe.wait_ge(const_loaded, 16 * N_CONST)
            pe.wait_ge(freed["X0"], 1)
            for t in range(4):
                mm = pe.transpose(bank["X0"][:, t * P:(t + 1) * P], vrows[:, t, :], ident[:])
            mm.then_inc(filled["X0"], 1)
            pe.wait_ge(cond_ready, 1)
            _, m, _ = plan.at[("init",)]
            with pe.Fori(0, MOD_INIT) as i:
                mod(i + m)
                mod_tail(i + m)
            for l in range(DEPTH):
                pre(l, 0)
                u, m, use = plan.at[(l, "win")]
                ready = xt_ready_at(l, 0)
                with pe.Fori(0, W_INC // 2) as i:
                    dense(i * 2 + u, "A", i + use["A0"], xt_hi, xt_lo, ready=ready, m=i + m, behind=IN_FIRST)
                    dense(i * 2 + (u + 1), "B", i + use["B0"], xt_hi, xt_lo, m=i + m, behind=IN_SECOND)
                    mod_tail(i + m)
                dense(u + W_INC - 1, "A", use["A0"] + W_INC // 2, xt_hi, xt_lo)
                z_complete(pe, l)
                got = attention(l)
                gates(l, 0)
                u, m, use = plan.at[(l, "out")]
                for step, banks in got.items():
                    if step[0] in ("value", "turn_c"):
                        for b, i in banks[-2:]:
                            read(b, i)
                with pe.Fori(0, ND // 2) as i:
                    dense(i * 2 + u, "A", i + use["A0"], xt_hi, xt_lo, m=i + m, behind=IN_FIRST)
                    dense(i * 2 + (u + 1), "B", i + use["B0"], xt_hi, xt_lo, m=i + m, behind=IN_SECOND)
                    mod_tail(i + m)
                pre(l, 1)
                for g, (c0, n) in enumerate(GROUPS):
                    u, m, use = plan.at[(l, "up", g)]
                    xr = xt_ready_at(l, 1)

                    def turn_hidden(i):
                        for s in range(2):
                            read(f"B{s}", i + use[f"B{s}"])
                            turn(f"X{s}", i + use[f"X{s}"], [hid[:, s, t * P:(t + 1) * P] for t in range(4)])

                    dense(u, "A", use["A0"], xt_hi, xt_lo, ready=xr)
                    first, second, one = (IN_FIRST, IN_SECOND, IN_ONE) if mod_up(l, g) else ({}, {}, {})
                    with pe.Fori(0, n - 1) as i:
                        dense(i * 2 + (u + 1), "B", i + use["B0"], xt_hi, xt_lo, m=i + m, behind=first)
                        dense(i * 2 + (u + 2), "A", i + (use["A0"] + 1), xt_hi, xt_lo, m=i + m, behind=second)
                        turn_hidden(i)
                        if mod_up(l, g):
                            mod_tail(i + m)
                    dense(u + 2 * n - 1, "B", use["B0"] + n - 1, xt_hi, xt_lo, m=m + n - 1, behind=one)
                    turn_hidden(n - 1)
                    if mod_up(l, g):
                        mod_tail(m + n - 1)
                    if g == 1:
                        gates(l, 1)

                    def hidden_ready(k):
                        if k % 4 == 0:
                            for s in range(2):
                                read(f"X{s}", use[f"X{s}"] + k // 4)

                    u, m, use2 = plan.at[(l, "down", g)]
                    if n == 4:
                        with pe.Fori(0, ND // 2) as i:
                            dense(i * 2 + u, "A", i + use2["A0"], ht_hi, ht_lo, ready=hidden_ready)
                            dense(i * 2 + (u + 1), "B", i + use2["B0"], ht_hi, ht_lo)
                    else:
                        for i in range(ND):
                            p = "AB"[i % 2]
                            with_mod = i < 2 and l + 1 < DEPTH
                            dense(u, p, use2[p + "0"] + i // 2, ht_hi, ht_lo, nk=4 * n, ph=2 * n * i, ready=hidden_ready,
                                  m=m, behind=(IN_FIRST, IN_SECOND)[i] if with_mod else {})
                            if with_mod and i == 1:
                                mod_tail(m)

        def ahead(split, u, ph=0, pieces=UNIT, between=None):
            for j in range(pieces):
                split(u, ph + LEAD + j)
                if between and j == pieces - 2:
                    between()

        def past_end(u, ph):
            return isinstance(u, int) and u * UNIT + ph >= TOTAL

        @block.scalar
        def _(act):
            n_sq = [0]
            n_hi = [0]

            def split(u, ph):
                if past_end(u, ph):
                    return
                act.wait_ge(raw_landed[ph % RING], u * (16 * UNIT // RING) + 16 * (ph // RING + 1))
                if not (isinstance(u, int) and u * UNIT + ph < RING):
                    act.wait_ge(w_used, u * UNIT + (ph - RING + 1))
                act.copy(whi[:, ph % RING], raw[:, ph % RING]).then_inc(hi_ready, 1)

            def fill_of(b, i):
                act.wait_ge(filled[b], plan.fill.get((b, i), i + 1) if isinstance(i, int) else i + 1)

            def square(src, dst):
                if n_sq[0]:
                    act.wait_ge(sq_ready, n_sq[0])
                n_sq[0] += 1
                act.activation(junk[:], src, ACT.Square, accum_out=dst).then_inc(sq_ready, 1)

            def high(dst, src):
                n_hi[0] += 1
                act.copy(dst, src).then_inc(hi_x, 1)

            def mod_row(i):
                act.wait_ge(mod_used, i * UNIT + UNIT)
                if not (isinstance(i, int) and i == 0):
                    act.wait_ge(filled["T"], i)
                act.copy(mrow[:], bank["M"][:]).then_inc(mrow_ready, 1)

            def squares(l, which):
                for n in range(ND):
                    for s in range(2):
                        if l or which:
                            act.wait_ge(x_new, 16 * l - 8 * (1 - which) + 2 * n + s + 1)
                        square(x[:, s, n * CH:(n + 1) * CH], ssx[:, s, n:n + 1])

            def pre(l, which):
                if l or which:
                    squares(l, which)
                act.wait_ge(vec_ready, 2 * l + which + 1)
                for b, uses in enumerate(plan.at[(l, "pre_uses", which)]):
                    bk, i = uses[1]
                    fill_of(bk, i)
                    if b > 1:
                        act.wait_ge(xt_ready, xt_count(l, which) - 8 + 2 * (b - 1))
                    for t in range(4):
                        k = 4 * b + t
                        ins = act.activation(xtmp[:, b % 2, 1, t, :], bank[bk][:, t * P:(t + 1) * P], ACT.Identity,
                                             scale=scal[:, k, 1:2], bias=shift[:, k, 1:2])
                    ins.then_inc(freed[bk], 1)
                    for s, (bk, i) in enumerate(uses):
                        act.wait_ge(freed[bk], i + 2)
                        high(xt_hi[:, 4 * b:4 * b + 4, s * P:(s + 1) * P], xtmp[:, b % 2, s])

            def gates(l, which):
                if which == 0:
                    act.wait_ge(kv_stored, 16 * 4 * (l + 1))
                for n, uses in enumerate(plan.at[(l, "gate_uses", which)]):
                    bk, i = uses[0]
                    fill_of(bk, i)
                    act.copy(gate[:, 0, n * CH:(n + 1) * CH], bank[bk][:]).then_inc(freed[bk], 1)

            def attention(l):
                for s in range(2):
                    if s == 0:
                        z_complete(act, l)
                    act.activation(z[:, s, U_C:W_IN], z[:, s, U_C:W_IN], ACT.Gelu_apprx_tanh).then_inc(gelu_ready, 1)
                for step, banks, m in plan.at[(l, "attention")]:
                    kind = step[0]
                    if kind == "mod_second":
                        mod_row(m)
                    elif kind in ("turn", "turn_ck", "turn_ws"):
                        b, i = banks[0]
                        dst = {"turn": qkt, "turn_ck": ckt, "turn_ws": wst}[kind]
                        j = step[-1] if kind != "turn_ws" else 0
                        if b == "X0":
                            fill_of(b, i)
                            act.copy(dst[:, 4 * j:4 * j + 4, :], four(bank[b][:])).then_inc(freed[b], 1)
                    elif kind == "score":
                        n = step[1]
                        s, ty = divmod(n, 2)
                        w = P * (1 + s)
                        act.wait_ge(nm_ready, 4 * l + n + 1)
                        for (b, i), heads in zip(banks, score_banks(n)):
                            for j, h in enumerate(heads):
                                dst = prob[:, n % 2, h, 0:w]
                                src = dst if n == 2 else bank[b][:, j * w:(j + 1) * w]
                                ins = act.activation(dst, src, ACT.Exp, bias=nmax[:, n, h:h + 1],
                                                     scale=1.0 if n == 2 else SCALE, accum_out=den[:, n, h:h + 1])
                            if n != 2:
                                ins.then_inc(freed[b], 1)
                        if ty:
                            ins = act.activation(esink[:, n, :], esink[:, n, :], ACT.Exp)
                        ins.then_inc(exp_ready, 1) if ty or n == 2 else exp_last(n)
                    elif kind == "value":
                        n = step[1]
                        s, ty = divmod(n, 2)
                        for j, (b, i) in enumerate(banks[:-2]):
                            if b == "X0":
                                fill_of(b, i)
                                k = min(4, NH * (1 + s) - 4 * j)
                                act.copy(pt[:, 4 * j:4 * j + k, :], four(bank[b][:])[:, 0:k, :]).then_inc(freed[b], 1)
                        for (b, i), heads in zip(banks[-2:], (range(0, 4), range(4, 6))):
                            fill_of(b, i)
                            k = len(heads)
                            k0 = ty * NH + heads[0]
                            high(xt_hi[:, k0:k0 + k, s * P:(s + 1) * P], four(bank[b][:])[:, 0:k, :])
                    elif kind == "turn_c":
                        s = step[1]
                        b, i = banks[0]
                        fill_of(b, i)
                        high(xt_hi[:, 12:16, s * P:(s + 1) * P], four(bank[b][:]))

            def exp_last(n):
                act.activation(esink[:, n, 0:1], nmax[:, n, 0:1], ACT.Copy).then_inc(exp_ready, 1)

            act.wait_ge(freed["X0"], 2)
            act.activation(silu_c[:].rearrange("p c t -> p (c t)"), vcols[:, 3 * P:3 * P + 2 * KD],
                           ACT.Silu).then_inc(silu_ready, 1)
            for j in range(LEAD):
                split(0, j)
            act.wait_ge(x_loaded, 32)
            squares(0, 0)
            _, m, _ = plan.at[("init",)]
            mod_row(m)
            with act.Fori(1, MOD_INIT) as i:
                mod_row(i + m)
            for l in range(DEPTH):
                pre(l, 0)
                u, m, _ = plan.at[(l, "win")]
                with act.Fori(0, W_INC // 2) as i:
                    ahead(split, i * 2 + u)
                    ahead(split, i * 2 + (u + 1), between=lambda: mod_row(i + m))
                ahead(split, u + W_INC - 1)
                attention(l)
                gates(l, 0)
                u, m, use = plan.at[(l, "out")]
                for i in range(ND):
                    ahead(split, u + i, between=(lambda: mod_row(m + i // 2)) if i % 2 else None)
                    act.wait_ge(w_used, (u + i + 1) * UNIT)
                    b = f"{'AB'[i % 2]}0"
                    act.copy(f[:, 0, i * CH:(i + 1) * CH], bank[b][:]).then_inc(freed[b], 1)
                    for s in range(2):
                        b = f"{'AB'[i % 2]}{s}"
                        act.wait_ge(freed[b], use[b] + i // 2 + 2)
                        square(f[:, s, i * CH:(i + 1) * CH], ssq[:, s, i:i + 1])
                pre(l, 1)
                for g, (c0, n) in enumerate(GROUPS):
                    u, m, use = plan.at[(l, "up", g)]

                    def silu(u, i, first=False):
                        act.wait_ge(w_used, u * UNIT + UNIT)
                        if not (first and g == 0 and l == 0):
                            act.wait_ge(freed["B1"], i + (use["B1"] + 1))
                        for s in range(2):
                            act.activation(sil[:, s, :], bank[f"A{s}"][:], ACT.Silu).then_inc(freed[f"A{s}"], 1)

                    def hidden_high(i):
                        for s in range(2):
                            act.wait_ge(filled[f"X{s}"], i + (use[f"X{s}"] + 1))
                            act.wait_ge(x_loaded, 32)
                            act.copy(ht_hi[:, bass.ds(i * 4, 4), s * P:(s + 1) * P],
                                     four(bank[f"X{s}"][:])).then_inc(ht_hi_ready, 1)

                    ahead(split, u)
                    silu(u, 0, True)
                    with act.Fori(0, n - 1) as i:
                        ahead(split, i * 2 + (u + 1))
                        ahead(split, i * 2 + (u + 2), between=(lambda: mod_row(i + m)) if mod_up(l, g) else None)
                        silu(i * 2 + (u + 2), i + 1)
                        hidden_high(i)
                    ahead(split, u + 2 * n - 1, between=(lambda: mod_row(m + n - 1)) if mod_up(l, g) else None)
                    hidden_high(n - 1)
                    if g == 1:
                        gates(l, 1)
                    u, m, use2 = plan.at[(l, "down", g)]
                    for i in range(ND):
                        if n == 4:
                            ahead(split, u + i)
                            act.wait_ge(w_used, (u + i + 1) * UNIT)
                        else:
                            ahead(split, u, 2 * n * i, 2 * n, (lambda: mod_row(m)) if i == 1 and l + 1 < DEPTH else None)
                            act.wait_ge(w_used, u * UNIT + 2 * n * (i + 1))
                        for s in range(2):
                            b = f"{'AB'[i % 2]}{s}"
                            if g == 0:
                                act.copy(f[:, s, i * CH:(i + 1) * CH], bank[b][:]).then_inc(freed[b], 1)
                            elif g == 2:
                                act.wait_ge(freed[b], use2[b] + i // 2 + 2)
                                square(f[:, s, i * CH:(i + 1) * CH], ssq[:, s, i:i + 1])

        @block.vector
        def _(dve):
            own = [0]
            n_hi = [0]

            def link(ins):
                own[0] += 1
                ins.then_inc(dve_own, 1)
                dve.wait_ge(dve_own, own[0])

            def split(u, ph):
                if past_end(u, ph):
                    return
                dve.wait_ge(hi_ready, u * UNIT + (ph + 1))
                if not (isinstance(u, int) and u * UNIT + ph < RING):
                    dve.wait_ge(w_used, u * UNIT + (ph - RING + 1))
                dve.tensor_tensor(wlo[:, ph % RING], raw[:, ph % RING], whi[:, ph % RING].bitcast(F32),
                                  ALU.subtract).then_inc(lo_ready, 1)

            def fill_of(b, i):
                dve.wait_ge(filled[b], plan.fill.get((b, i), i + 1) if isinstance(i, int) else i + 1)

            def mod_cols(i):
                dve.wait_ge(filled["T"], i + 1)
                dve.tensor_scalar(modt[:, bass.ds(i * 8, 8)], bank["T"][:, 0:8], 1.0, None, ALU.mult).then_inc(freed["T"], 1)

            def mean_square(sums, j):
                dve.wait_ge(sq_ready, 8 * j)
                link(dve.tensor_reduce(msum[:], sums, AX_X, ALU.add))
                dve.tensor_scalar(ms[:], msum[:], 1.0 / D, EPS, ALU.mult, ALU.add).then_inc(ms_ready, 1)
                dve.wait_ge(rstd_ready, j)

            def low(dst, src, hi, s_out):
                n_hi[0] += 1
                dve.wait_ge(hi_x, n_hi[0])
                dve.tensor_tensor(dst, src, hi.bitcast(F32), ALU.subtract).then_inc(s_out, 1)

            def norm_vectors(l, which):
                v = 3 * which
                dve.wait_ge(freed["T"], mod_done(l, v + 1) + 1)
                link(dve.tensor_tensor(scal[:], mod_t(l, v + 1), mod_b(l, v + 1), ALU.add))
                dve.tensor_tensor(shift[:], mod_t(l, v), mod_b(l, v), ALU.add)
                dve.scalar_tensor_tensor(out=scal[:], in0=scal[:], scalar=1.0, in1=vec(2 * which, l),
                                         op0=ALU.add, op1=ALU.mult).then_inc(vec_ready, 1)

            def normalise(l, which):
                mean_square(ssx[:], 4 * l + 2 * which + 1)
                for s in range(2):
                    dve.tensor_scalar(f[:, s, :], x[:, s, :], rstd[:, s:s + 1], None, ALU.mult).then_inc(xn_ready, 1)

            def pre(l, which):
                dve.wait_ge(vec_ready, 2 * l + which + 1)

                def lows(b):
                    for s in range(2):
                        t = (slice(None), slice(4 * b, 4 * b + 4), slice(s * P, (s + 1) * P))
                        low(xt_lo[t], xtmp[:, b % 2, s], xt_hi[t], xt_ready)

                for b, uses in enumerate(plan.at[(l, "pre_uses", which)]):
                    bk, i = uses[0]
                    fill_of(bk, i)
                    if b > 1:
                        dve.wait_ge(xt_ready, xt_count(l, which) - 8 + 2 * (b - 1))
                    for t in range(4):
                        k = 4 * b + t
                        ins = dve.tensor_scalar(xtmp[:, b % 2, 0, t, :], bank[bk][:, t * P:(t + 1) * P], scal[:, k, 0:1],
                                                shift[:, k, 0:1], ALU.mult, ALU.add)
                    ins.then_inc(freed[bk], 1)
                    if b:
                        lows(b - 1)
                lows(b)

            def gate_vector(l, which):
                v = 3 * which + 2
                dve.wait_ge(freed["T"], mod_done(l, v) + 1)
                link(dve.tensor_tensor(gatev[:], mod_t(l, v), mod_b(l, v), ALU.add))
                dve.tensor_tensor(gatev[:], gatev[:], vec(2 * which + 1, l), ALU.mult).then_inc(gate_ready, 1)

            def gates(l, which):
                if which == 0:
                    dve.wait_ge(kv_stored, 16 * 4 * (l + 1))
                for n, uses in enumerate(plan.at[(l, "gate_uses", which)]):
                    bk, i = uses[1]
                    fill_of(bk, i)
                    dve.tensor_copy(gate[:, 1, n * CH:(n + 1) * CH], bank[bk][:]).then_inc(freed[bk], 1)

            def post(l, which):
                mean_square(ssq[:], 4 * l + 2 * which + 2)
                for n in range(ND):
                    c = slice(n * CH, (n + 1) * CH)
                    for s in range(2):
                        dve.scalar_tensor_tensor(out=x[:, s, c], in0=f[:, s, c], scalar=rstd[:, s:s + 1], in1=x[:, s, c],
                                                 op0=ALU.mult, op1=ALU.add).then_inc(x_new, 1)

            def gated(l, which, n):
                for s in range(2):
                    bk, i = plan.at[(l, "gate_uses", which)][n][s]
                    dve.wait_ge(freed[bk], i + 2)
                    dve.wait_ge(sq_ready, 8 * (4 * l + 2 * which + 1) + 2 * n + s + 1)
                    c = slice(n * CH, (n + 1) * CH)
                    ins = dve.tensor_tensor(f[:, s, c], f[:, s, c], gate[:, s, c], ALU.mult)
                link(ins)

            def attention(l):
                dve.wait_ge(att_loaded, 16 * N_ATT * (l + 1))
                dve.tensor_tensor(bias[:], bias[:], edge[:].unsqueeze(1).broadcast_to([P, NH, P]), ALU.add)
                link(dve.tensor_scalar(nsink[:], sink[:], -1.0, None, ALU.mult))
                for step, banks, m in plan.at[(l, "attention")]:
                    kind = step[0]
                    if kind == "mod_tail":
                        mod_cols(m)
                    elif kind in ("turn", "turn_ck", "turn_ws"):
                        b, i = banks[0]
                        dst = {"turn": qkt, "turn_ck": ckt, "turn_ws": wst}[kind]
                        j = step[-1] if kind != "turn_ws" else 0
                        if b == "X1":
                            fill_of(b, i)
                            dve.tensor_copy(dst[:, 4 * j:4 * j + 4, :], four(bank[b][:])).then_inc(freed[b], 1)
                    elif kind == "score":
                        n = step[1]
                        s, ty = divmod(n, 2)
                        w = P * (1 + s)
                        for (b, i), heads in zip(banks, score_banks(n)):
                            fill_of(b, i)
                            k = len(heads)
                            sc = bank[b][:, 0:k * w].rearrange("p (h w) -> p h w", w=w)
                            hs = slice(heads[0], heads[0] + k)
                            if n == 2:
                                dve.scalar_tensor_tensor(out=prob[:, 0, hs, 0:P], in0=sc[:, :, 0:P], scalar=SCALE,
                                                         in1=bias[:, hs, :], op0=ALU.mult, op1=ALU.add)
                                ins = dve.tensor_scalar(prob[:, 0, hs, P:w], sc[:, :, P:w], SCALE, None, ALU.mult)
                                ins.then_inc(freed[b], 1)
                            else:
                                ins = dve.tensor_reduce(rmax[:, n, hs], sc, AX_X, ALU.max)
                        if n == 2:
                            dve.wait_ge(freed[b], i + 2)
                            ins = dve.tensor_reduce(rmax[:, n, :], prob[:, 0, :, :], AX_X, ALU.max)
                        link(ins)
                        if ty:
                            link(dve.scalar_tensor_tensor(out=nmax[:, n, :], in0=rmax[:, n, :], scalar=-SCALE,
                                                          in1=nsink[:], op0=ALU.mult, op1=ALU.min))
                            dve.tensor_tensor(esink[:, n, :], nmax[:, n, :], sink[:], ALU.add).then_inc(nm_ready, 1)
                        else:
                            dve.tensor_scalar(nmax[:, n, :], rmax[:, n, :], -1.0 if n == 2 else -SCALE, None,
                                              ALU.mult).then_inc(nm_ready, 1)
                    elif kind == "soft":
                        n = step[1]
                        s, ty = divmod(n, 2)
                        w = P * (1 + s)
                        dve.wait_ge(exp_ready, 4 * l + n + 1)
                        if ty:
                            link(dve.tensor_tensor(den[:, n, :], den[:, n, :], esink[:, n, :], ALU.add))
                        link(dve.reciprocal(den[:, n, :], den[:, n, :]))
                        pr = prob[:, n % 2, :, 0:w]
                        dve.tensor_tensor(pr, pr, den[:, n, :].unsqueeze(2).broadcast_to([P, NH, w]),
                                          ALU.mult).then_inc(pn_ready, 1)
                    elif kind == "value":
                        n = step[1]
                        s, ty = divmod(n, 2)
                        for j, (b, i) in enumerate(banks[:-2]):
                            if b == "X1":
                                fill_of(b, i)
                                k = min(4, NH * (1 + s) - 4 * j)
                                dve.tensor_copy(pt[:, 4 * j:4 * j + k, :], four(bank[b][:])[:, 0:k, :]).then_inc(freed[b], 1)
                        for (b, i), heads in zip(banks[-2:], (range(0, 4), range(4, 6))):
                            k = len(heads)
                            k0 = ty * NH + heads[0]
                            t = (slice(None), slice(k0, k0 + k), slice(s * P, (s + 1) * P))
                            low(xt_lo[t], four(bank[b][:])[:, 0:k, :], xt_hi[t], freed[b])
                    elif kind == "norm_v":
                        s = step[1]
                        v = z[:, s, V_C:W_IN]
                        dve.wait_ge(gelu_ready, 2 * l + s + 1)
                        link(dve.bn_stats(vstat[:, s, :], v))
                        link(dve.bn_aggr(vmv[:, s, :], vstat[:, s, :]))
                        dve.tensor_scalar(vmv[:, s, 1:2], vmv[:, s, 1:2], EPS, None, ALU.add).then_inc(vmv_ready, 1)
                        dve.wait_ge(vrstd_ready, 2 * l + s + 1)
                        link(dve.tensor_scalar(v, v, vmv[:, s, 0:1], vrstd[:, s:s + 1], ALU.subtract, ALU.mult))
                        link(dve.tensor_tensor(v, v, ln_g[:], ALU.mult))
                        dve.tensor_tensor(v, v, ln_b, ALU.add).then_inc(vn_ready, 1)
                    elif kind == "gate_c":
                        s = step[1]
                        b, i = banks[0]
                        fill_of(b, i)
                        for g in range(GC):
                            ug = z[:, s, U_C + g * P:U_C + (g + 1) * P]
                            c = 3 * P + 2 * KD + l * GC + g
                            ins = dve.scalar_tensor_tensor(out=ug, in0=bank[b][:, g * P:(g + 1) * P],
                                                           scalar=vcols[:, c:c + 1], in1=ug, op0=ALU.add, op1=ALU.mult)
                        ins.then_inc(freed[b], 1)
                    elif kind == "turn_c":
                        s = step[1]
                        b, i = banks[0]
                        t = (slice(None), slice(12, 16), slice(s * P, (s + 1) * P))
                        low(xt_lo[t], four(bank[b][:]), xt_hi[t], freed[b])

            dve.memset(vrows, 0.0).then_inc(vrows_clear, 1)
            dve.memset(minus_half[:], -0.5)
            dve.memset(cond[:, 2 * KD:], 0.0)
            for b in BANKS:
                dve.memset(clear[:, BANKS.index(b):BANKS.index(b) + 1], 0.0).then_inc(freed[b], 1)
            fill_of("X0", 0)
            dve.tensor_copy(vcols[:], bank["X0"][:]).then_inc(freed["X0"], 1)
            dve.wait_ge(silu_ready, 1)
            dve.tensor_copy(cond[:, 0:2 * KD].rearrange("p (t c) -> p t c", c=2),
                            silu_c[:].rearrange("p c t -> p t c")).then_inc(cond_ready, 1)
            for j in range(LEAD):
                split(0, j)
            normalise(0, 0)
            u, m, _ = plan.at[("init",)]
            with dve.Fori(0, MOD_INIT) as i:
                mod_cols(i + m)
            for l in range(DEPTH):
                if l == 0:
                    norm_vectors(l, 0)
                pre(l, 0)
                u, m, use = plan.at[(l, "win")]

                def read_out(u, col, pair):
                    dve.wait_ge(w_used, u * UNIT + UNIT)
                    for s in range(2):
                        dve.tensor_scalar(z[:, s, bass.ds(col, CH)], bank[f"{pair}{s}"][:], 1.0, None,
                                          ALU.mult).then_inc(freed[f"{pair}{s}"], 1)

                with dve.Fori(0, W_INC // 2) as i:
                    ahead(split, i * 2 + u)
                    read_out(i * 2 + u, i * 2 * CH, "A")
                    ahead(split, i * 2 + (u + 1))
                    read_out(i * 2 + (u + 1), i * 2 * CH + CH, "B")
                    mod_cols(i + m)
                ahead(split, u + W_INC - 1)
                read_out(u + W_INC - 1, (W_INC - 1) * CH, "A")
                gate_vector(l, 0)
                attention(l)
                gates(l, 0)
                u, m, use = plan.at[(l, "out")]
                for i in range(ND):
                    ahead(split, u + i)
                    dve.wait_ge(w_used, (u + i + 1) * UNIT)
                    b = f"{'AB'[i % 2]}1"
                    dve.tensor_copy(f[:, 1, i * CH:(i + 1) * CH], bank[b][:]).then_inc(freed[b], 1)
                    if i % 2:
                        mod_cols(m + i // 2)
                    gated(l, 0, i)
                norm_vectors(l, 1)
                post(l, 0)
                normalise(l, 1)
                pre(l, 1)
                for g, (c0, n) in enumerate(GROUPS):
                    u, m, use = plan.at[(l, "up", g)]

                    def multiply(u, i):
                        dve.wait_ge(w_used, u * UNIT + UNIT)
                        dve.wait_ge(filled["X1"], i + use["X1"])
                        for s in range(2):
                            dve.wait_ge(freed[f"A{s}"], i + (use[f"A{s}"] + 2))
                            dve.tensor_tensor(hid[:, s, :], sil[:, s, :], bank[f"B{s}"][:],
                                              ALU.mult).then_inc(freed[f"B{s}"], 1)

                    def hidden_low(i, first):
                        for s in range(2):
                            dve.wait_ge(ht_hi_ready, i * 2 + (first + s + 1))
                            t = (slice(None), bass.ds(i * 4, 4), slice(s * P, (s + 1) * P))
                            dve.tensor_tensor(ht_lo[t], four(bank[f"X{s}"][:]), ht_hi[t].bitcast(F32),
                                              ALU.subtract).then_inc(freed[f"X{s}"], 1)

                    first = 2 * (FFC * l + c0)
                    ahead(split, u)
                    with dve.Fori(0, n - 1) as i:
                        ahead(split, i * 2 + (u + 1))
                        multiply(i * 2 + (u + 1), i)
                        ahead(split, i * 2 + (u + 2))
                        hidden_low(i, first)
                        if mod_up(l, g):
                            mod_cols(i + m)
                    ahead(split, u + 2 * n - 1)
                    multiply(u + 2 * n - 1, n - 1)
                    hidden_low(n - 1, first)
                    if mod_up(l, g):
                        mod_cols(m + n - 1)
                    if g == 0:
                        gate_vector(l, 1)
                    if g == 1:
                        gates(l, 1)
                    u, m, use2 = plan.at[(l, "down", g)]
                    for i in range(ND):
                        if n == 4:
                            ahead(split, u + i)
                            dve.wait_ge(w_used, (u + i + 1) * UNIT)
                        else:
                            ahead(split, u, 2 * n * i, 2 * n)
                            dve.wait_ge(w_used, u * UNIT + 2 * n * (i + 1))
                        for s in range(2):
                            b = f"{'AB'[i % 2]}{s}"
                            if g:
                                c = slice(i * CH, (i + 1) * CH)
                                dve.tensor_tensor(f[:, s, c], f[:, s, c], bank[b][:], ALU.add).then_inc(freed[b], 1)
                        if g == len(GROUPS) - 1:
                            if i == 1 and l + 1 < DEPTH:
                                mod_cols(m)
                            gated(l, 1, i)
                if l + 1 < DEPTH:
                    norm_vectors(l + 1, 0)
                post(l, 1)
                if l + 1 < DEPTH:
                    normalise(l + 1, 0)


_INS = ['x_prompt', 'x_sample', 'cache_a_k', 'cache_a_v', 'cache_b_k', 'cache_b_v', 'c', 'c_ctx', 'mod_w', 'mod_b',
        'norm_mix_pre', 'norm_mix_post', 'norm_ffn_pre', 'norm_ffn_post', 'w_in', 'w_out', 'rpb_a', 'sink_b',
        'gmlp_ln_g', 'gmlp_ln_b', 'gmlp_w', 'gmlp_b', 'w_gate', 'w_up', 'w_down']
_OUTS = [(1, 128, 2048), (1, 128, 2048), (1, 2, 6, 128, 128), (1, 2, 6, 128, 128), (1, 2, 2, 128, 128), (1, 2, 2, 128, 128)]


def constants():
    t = np.arange(P)
    half = 32
    freqs = (np.float32(10000.0) ** (-np.arange(half, dtype=np.float32) / np.float32(half))).astype(np.float32)
    rope = np.zeros((P, 2, 2, 2, half), np.float32)
    for axis, pos in enumerate((t // GRID, t % GRID)):
        ang = pos.astype(np.float32)[:, None] * freqs[None, :]
        rope[:, 0, axis, 0] = rope[:, 0, axis, 1] = np.cos(ang)
        rope[:, 1, axis, 0] = -np.sin(ang)
        rope[:, 1, axis, 1] = np.sin(ang)
    col = t % GRID
    c0 = np.clip(col - 8, 0, GRID - 16)
    ok = (col[None, :] >= c0[:, None]) & (col[None, :] < c0[:, None] + 16)
    rsel = np.zeros((P, 2), np.float32)
    rsel[0::32, 0] = rsel[1::32, 1] = 1
    return {
        "c_ident": np.eye(P, dtype=np.float32), "c_rsel": rsel, "c_rope": rope.reshape(P, 2 * P),
        "c_edge": np.where(ok, 0, NEG).astype(np.float32),
        "c_zero": np.zeros((DEPTH * NH * 3, 2 * GRID - 1), np.float32),
    }


def kernel(**inputs):
    import concourse.bacc as bacc
    from concourse.bass_utils import run_bass_kernel_spmd

    nc = bacc.Bacc("TRN2", target_bir_lowering=False, num_devices=1)
    arrays, args = {}, {}
    for name, v in [(n, inputs[n]) for n in _INS] + list(constants().items()):
        v = np.ascontiguousarray(v)
        arrays[f"in_{name}"] = v
        args[name] = nc.dram_tensor(f"in_{name}", v.shape, F32, kind="ExternalInput").ap()
    for i, shape in enumerate(_OUTS):
        args[f"out_{i}"] = nc.dram_tensor(f"out_{i}", shape, F32, kind="ExternalOutput").ap()
    build_program(nc, args)
    r = run_bass_kernel_spmd(nc, [arrays], core_ids=[0])
    return tuple(r.results[0][f"out_{i}"] for i in range(len(_OUTS)))
```

```python
from contextlib import ExitStack

import numpy as np

import concourse.bass as bass
from concourse import mybir

F32 = mybir.dt.float32
F32R = mybir.dt.float32r
ALU = mybir.AluOpType
ACT = mybir.ActivationFunctionType
AX_X = mybir.AxisListType.X

P = 128
D = 2048
KD = D // P
DEPTH = 2
CH = 512
ND = D // CH
NH = 6
KVB = 2
GC = 4
W_IN = 4608
W_INC = W_IN // CH
Q_A, K_A, V_A, Q_B, K_B, V_B, U_C, V_C = 0, 768, 1536, 2304, 3072, 3328, 3584, 4096
FF = 5632
FFC = FF // CH
GROUPS = [(0, 4), (4, 4), (8, 3)]
NMODC = 6 * D // CH
SCALE = float(P) ** -0.5
EPS = 1e-6
NEG = -1e30
GRID = 64

KB = 2
UNIT = KD // KB
RING = 4
LEFT = 2
LEAD = 4
IN_ONE = {1: range(0, 4), 5: range(4, 8)}
IN_FIRST, IN_SECOND = {3: range(0, 4)}, {3: range(4, 8)}
LOAD_ONE = {0: [0], 1: [1], 2: [2], 3: [3], 4: [4], 5: [5], 6: [6], 7: [7]}
LOAD_FIRST, LOAD_SECOND = ({0: [j], 2: [j + 1], 4: [j + 2], 6: [j + 3]} for j in (0, 4))

MOD_INIT = 2 * ND
MOD_WIN = W_INC // 2
MOD_OUT = ND // 2


def mod_up(l, g):
    return g == 0 or l + 1 < DEPTH

GELU_BEFORE = [("turn_ck", 1), ("turn", 1, 1)]
BANKS = ["A0", "A1", "B0", "B1", "M", "X0", "X1", "T"]


def attention_steps():
    def mods(*parts):
        return [(f"mod_{p}",) for p in parts]
    s = mods("first") + [("turn", 0, b) for b in range(5)] + mods("second")
    s += [("score", 0), ("turn_ws",), ("turn_ck", 0), ("turn_ck", 1)] + mods("tail", "first")
    s += [("score", 1)] + [("turn", 1, b) for b in range(3)] + [("soft", 0)] + mods("second")
    s += [("norm_v", 0), ("turn", 1, 3), ("turn", 1, 4), ("value", 0), ("soft", 1)] + mods("tail", "first")
    s += [("score", 2), ("norm_v", 1)] + mods("second") + [("value", 1)] + mods("tail", "first")
    s += [("score", 3), ("soft", 2), ("gate_c", 0), ("gate_c", 1)] + mods("second")
    s += [("value", 2), ("soft", 3), ("turn_c", 0), ("turn_c", 1)] + mods("tail", "first")
    s += [("value", 3)] + mods("second", "tail")
    return s


def start_piece(q):
    n, i = divmod(q, 4)
    return n, i // 2, 2 * n + i % 2


def start_chunk(m):
    return (m % 2) * ND + m // 2


def score_banks(n):
    return [range(0, 4), range(4, 6)] if n < 2 else [range(0, 2), range(2, 4), range(4, 6)]


class Plan:

    def __init__(self):
        self.unit, self.mod, self.use = 0, 0, dict.fromkeys(BANKS, 0)
        self.fills, self.fill = dict.fromkeys(BANKS, 0), {}
        self.at = {}
        self.turn_bank = 0
        self.acc_bank = 0

        self.mark(("init",))
        self.take("X0")
        self.mods(MOD_INIT)
        for l in range(DEPTH):
            self.pre(l, 0)
            self.mark((l, "win"))
            self.unit += W_INC
            self.mods(MOD_WIN)
            self.takes(["A0", "A1"], (W_INC + 1) // 2)
            self.takes(["B0", "B1"], W_INC // 2)
            self.mark((l, "att"))
            self.attention(l)
            self.gate(l, 0)
            self.mark((l, "out"))
            self.unit += ND
            self.takes(["A0", "A1", "B0", "B1"], ND // 2)
            self.mods(MOD_OUT + 1)
            self.pre(l, 1)
            for g, (_, n) in enumerate(GROUPS):
                self.mark((l, "up", g))
                self.unit += 2 * n
                self.takes(["A0", "A1", "B0", "B1", "X0", "X1"], n)
                if mod_up(l, g):
                    self.mods(n)
                if g == 1:
                    self.gate(l, 1)
                self.mark((l, "down", g))
                self.unit += n if n < 4 else ND
                self.takes(["A0", "A1", "B0", "B1"], ND // 2)
            self.mark((l, "mod_pre_mix"))
            if l + 1 < DEPTH:
                self.mods(1)

    def mark(self, key):
        self.at[key] = (self.unit, self.mod, dict(self.use))

    def mods(self, n):
        self.mod += n
        self.takes(["M", "T"], n)

    def takes(self, banks, n):
        for b in banks:
            self.use[b] += n
            if b in ("X0", "X1", "T"):
                self.fills[b] += n

    def take(self, bank):
        self.use[bank] += 1
        self.fills[bank] += 1
        self.fill[(bank, self.use[bank] - 1)] = self.fills[bank]
        return bank, self.use[bank] - 1

    def turn(self):
        self.turn_bank ^= 1
        return self.take(("X0", "X1")[self.turn_bank])

    def acc(self):
        self.acc_bank = (self.acc_bank + 1) % 4
        return self.take(BANKS[self.acc_bank])

    def pre(self, l, which):
        self.mark((l, "pre", which))
        self.at[(l, "pre_uses", which)] = [[self.take(f"X{s}") for s in range(2)] for _ in range(KD // 4)]

    def gate(self, l, which):
        self.at[(l, "gate_uses", which)] = [[self.take(f"X{s}") for s in range(2)] for _ in range(ND)]

    def attention(self, l):
        uses = []
        for step in attention_steps():
            mine = self.mod
            banks = []
            if step[0] in ("turn", "turn_ck", "turn_ws", "turn_c"):
                banks = [self.turn()]
            elif step[0] == "score":
                banks = [self.acc() for _ in score_banks(step[1])]
            elif step[0] == "value":
                banks = [self.turn() for _ in range(2 if step[1] < 2 else 3)] + [self.acc() for _ in range(2)]
            elif step[0] == "gate_c":
                banks = [self.acc()]
            elif step[0] == "mod_first":
                self.mods(1)
            uses.append((step, banks, mine if step[0] == "mod_first" else mine - 1))
        self.at[(l, "attention")] = uses


def build_program(nc, a):
    plan = Plan()
    TOTAL = plan.unit * UNIT
    xin = [a["x_prompt"][0], a["x_sample"][0]]
    xout = [a["out_0"][0], a["out_1"][0]]

    def four(ap):
        return ap.rearrange("p (t c) -> p t c", t=4)

    with ExitStack() as ctx:
        def sem(name):
            return ctx.enter_context(nc.semaphore(name))

        def sb(name, shape, dt=F32, at=ctx):
            return at.enter_context(nc.sbuf_tensor(name, shape, dt))

        bank = {b: ctx.enter_context(nc.psum_tensor(f"bank_{b}", [P, CH], F32)) for b in BANKS}

        raw = sb("raw", [P, RING, KB, CH])
        mraw = sb("mraw", [P, RING, KB, CH])
        whi = sb("whi", [P, RING, KB, CH], F32R)
        wlo = sb("wlo", [P, RING, KB, CH], F32R)
        x = sb("x", [P, 2, D])
        xt_hi = sb("xt_hi", [P, KD, 2 * P], F32R)
        xt_lo = sb("xt_lo", [P, KD, 2 * P], F32R)
        ident = sb("ident", [P, P])
        rsel = sb("rsel", [P, 2])
        rope = sb("rope", [P, 2, P])
        edge = sb("edge", [P, P])
        vcols = sb("vcols", [P, 4 * P])
        silu_c = sb("silu_c", [P, 2, KD])
        cond = sb("cond", [P, KD * 2 + 32])
        mrow = sb("mrow", [P, CH])
        modt = sb("modt", [P, DEPTH * NMODC * 8])
        shift = sb("shift", [P, KD, 2])
        scal = sb("scal", [P, KD, 2])
        gatev = sb("gatev", [P, KD, 2])
        ssq = sb("ssq", [P, 2, ND])
        ssx = sb("ssx", [P, 2, ND])
        ms = sb("ms", [P, 2])
        rstd = sb("rstd", [P, 2])
        minus_half = sb("minus_half", [P, 2])
        junk = sb("junk", [P, CH])

        ffn = ExitStack()
        gate = sb("gate", [P, 2, D], F32, ffn)
        ht_hi = sb("ht_hi", [P, KD, 2 * P], F32R, ffn)
        ht_lo = sb("ht_lo", [P, KD, 2 * P], F32R, ffn)
        f = sb("f", [P, 2, D], F32, ffn)
        hid = sb("hid", [P, 2, CH], F32, ffn)
        sil = sb("sil", [P, 2, CH], F32, ffn)
        xtmp = sb("xtmp", [P, 2, 2, 4, P], F32, ffn)
        ffn.close()
        z = sb("z", [P, 2, W_IN])
        qkt = sb("qkt", [P, 20, P])
        cv = sb("cv", [P, NH + KVB, P])
        ckt = sb("ckt", [P, NH + KVB, P])
        bias = sb("bias", [P, NH, P])
        turned_b = sb("turned_b", [P, 8, P])
        prob = sb("prob", [P, 2, NH, 2 * P])
        pt = sb("pt", [P, 12, P])
        ln_g = sb("ln_g", [P, CH])
        vrows = four(z[:, 0, 0:4 * P])
        late = prob[:, 1].rearrange("p h c -> p (h c)").rearrange("p (t c) -> p t c", c=P)
        ck, ws = late[:, 0:8, :], late[:, 8:12, :]
        crossed, ln_b = pt[:, 0:8, :], pt[:, 8:12, :].rearrange("p t c -> p (t c)")
        wst = sb("wst", [P, GC, P])
        sink = sb("sink", [P, NH])
        nsink = sb("nsink", [P, NH])
        msum = sb("msum", [P, 2])
        clear = sb("clear", [P, len(BANKS)])
        rmax = sb("rmax", [P, 4, NH])
        nmax = sb("nmax", [P, 4, NH])
        den = sb("den", [P, 4, NH])
        esink = sb("esink", [P, 4, NH])
        vstat = sb("vstat", [P, 2, 6])
        vmv = sb("vmv", [P, 2, 2])
        vrstd = sb("vrstd", [P, 2])

        PADW = 2 * GRID - 1
        rpb_pad = nc.dram_tensor("rpb_pad", [DEPTH * NH * 3, PADW], F32, kind="Internal").ap()
        rpb_rows = nc.dram_tensor("rpb_rows", [GRID, DEPTH * NH * 3, PADW], F32, kind="Internal").ap()

        filled = {b: sem(f"filled_{b}") for b in BANKS}
        freed = {b: sem(f"freed_{b}") for b in BANKS}
        raw_landed = [sem(f"raw_landed_{i}") for i in range(RING)]
        mraw_landed = [sem(f"mraw_landed_{i}") for i in range(RING)]
        mod_used = sem("mod_used")
        hi_ready = sem("hi_ready")
        lo_ready = sem("lo_ready")
        w_used = sem("w_used")
        const_loaded = sem("const_loaded")
        x_loaded = sem("x_loaded")
        pad_cleared = sem("pad_cleared")
        pad_filled = sem("pad_filled")
        pad_copied = sem("pad_copied")
        att_loaded = sem("att_loaded")
        vrows_clear = sem("vrows_clear")
        silu_ready = sem("silu_ready")
        cond_ready = sem("cond_ready")
        dve_own = sem("dve_own")
        pool_own = sem("pool_own")
        mrow_ready = sem("mrow_ready")
        xt_ready = sem("xt_ready")
        vec_ready = sem("vec_ready")
        sq_ready = sem("sq_ready")
        ms_ready = sem("ms_ready")
        rstd_ready = sem("rstd_ready")
        xn_ready = sem("xn_ready")
        gate_ready = sem("gate_ready")
        hi_x = sem("hi_x")
        x_new = sem("x_new")
        ht_hi_ready = sem("ht_hi_ready")
        gelu_ready = sem("gelu_ready")
        rope_ready = sem("rope_ready")
        nm_ready = sem("nm_ready")
        exp_ready = sem("exp_ready")
        pn_ready = sem("pn_ready")
        vmv_ready = sem("vmv_ready")
        vrstd_ready = sem("vrstd_ready")
        vn_ready = sem("vn_ready")
        kv_stored = sem("kv_stored")
        x_stored = sem("x_stored")

        def vec(v, l):
            c = (v * DEPTH + l) * KD
            return vcols[:, c:c + KD].unsqueeze(2).broadcast_to([P, KD, 2])

        def mod_b(l, v):
            c = P * (1 + l) + v * KD
            return vcols[:, c:c + KD].unsqueeze(2).broadcast_to([P, KD, 2])

        def mod_t(l, v):
            c = (l * 6 + v) * KD * 2
            return modt[:, c:c + KD * 2].rearrange("p (t c) -> p t c", c=2)

        def mod_done(l, v):
            return l * NMODC + (v + 1) * ND

        def xt_count(l, which):
            return 16 * l + 8 * (which + 1)

        def z_complete(engine, l):
            for b in ("A0", "A1", "B0", "B1"):
                engine.wait_ge(freed[b], plan.at[(l, "att")][2][b] + 1)

        def vec_count(l, which):
            return 2 * l + which + ND

        N_CONST = 13
        N_ATT = 12

        block = ctx.enter_context(nc.Block())

        @block.sync
        def _(sp):
            def piece(u, ph, src):
                if not (isinstance(u, int) and u * UNIT + ph < RING):
                    sp.wait_ge(lo_ready, u * UNIT + (ph - RING + 1))
                sp.dma_start(raw[:, ph % RING], src.rearrange("(t p) n -> p t n", p=P)).then_inc(
                    raw_landed[ph % RING], 16)

            def chunk(u, w, row0, col, pieces=UNIT, ph=0):
                for j in range(pieces):
                    piece(u, ph + j, w[row0 + j * KB * P:row0 + (j + 1) * KB * P, bass.ds(col, CH)])

            def mod_chunk(m, l, js=range(UNIT), col=None):
                for j in js:
                    if not (isinstance(m, int) and m * UNIT + j < RING):
                        sp.wait_ge(mod_used, m * UNIT + (j - RING + 1))
                    src = a["mod_w"][l, j * KB * P:(j + 1) * KB * P, bass.ds((m - l * NMODC if col is None else col) * CH, CH)]
                    sp.dma_start(mraw[:, j % RING], src.rearrange("(t p) n -> p t n", p=P)).then_inc(
                        mraw_landed[j % RING], 16)

            def both(u, w, col, m=0, l=0, behind={}, js=range(UNIT)):
                for j in js:
                    piece(u, j, w[j * KB * P:(j + 1) * KB * P, bass.ds(col, CH)])
                    if j in behind:
                        mod_chunk(m, l, behind[j])

            def first_unit(u, w, col):
                both(u, w, col, js=range(LEAD))

            def both_rest(u, w, col, m, l):
                for j in range(LEAD):
                    mod_chunk(m, l, LOAD_FIRST.get(j, []))
                both(u, w, col, m, l, LOAD_FIRST, range(LEAD, UNIT))

            def start_load(q):
                _, c, j = start_piece(q)
                piece(0, q, a["w_in"][0, j * KB * P:(j + 1) * KB * P, c * CH:(c + 1) * CH])

            for m in range(MOD_INIT):
                for h in range(2):
                    mod_chunk(m, 0, range(4 * h, 4 * h + 4), start_chunk(m))
                    if m == h == 0:
                        for q in range(LEAD):
                            start_load(q)
                    elif m > 1:
                        start_load(2 * m + h)
            for l in range(DEPTH):
                u, m, _ = plan.at[(l, "win")]
                w = a["w_in"][l]
                if l:
                    both_rest(u, w, 0, m, l)
                    both(u + 1, w, CH, m, l, LOAD_SECOND)
                else:
                    m -= 1
                with sp.Fori(1, W_INC // 2) as i:
                    both(i * 2 + u, w, i * 2 * CH, i + m, l, LOAD_FIRST)
                    both(i * 2 + (u + 1), w, i * 2 * CH + CH, i + m, l, LOAD_SECOND)
                both(u + W_INC - 1, w, (W_INC - 1) * CH, m + W_INC // 2, l, {} if l else LOAD_ONE)
                u, m, _ = plan.at[(l, "out")]
                w = a["w_out"][l]
                first_unit(u, w, 0)
                for step, _, m_att in plan.at[(l, "attention")]:
                    if step[0] == "mod_first":
                        mod_chunk(m_att, l)
                both_rest(u, w, 0, m, l)
                both(u + 1, w, CH, m, l, LOAD_SECOND)
                with sp.Fori(1, ND // 2) as i:
                    both(i * 2 + u, w, i * 2 * CH, i + m, l, LOAD_FIRST)
                    both(i * 2 + (u + 1), w, i * 2 * CH + CH, i + m, l, LOAD_SECOND)
                first_unit(plan.at[(l, "up", 0)][0], a["w_gate"][l], 0)
                mod_chunk(m + MOD_OUT, l)
                for g, (c0, n) in enumerate(GROUPS):
                    u, m, _ = plan.at[(l, "up", g)]
                    lm = l + (g > 0)
                    both(u, a["w_gate"][l], c0 * CH, js=range(0 if g else LEAD, UNIT))
                    with sp.Fori(0, n - 1) as i:
                        if mod_up(l, g):
                            both(i * 2 + (u + 1), a["w_up"][l], i * CH + c0 * CH, i + m, lm, LOAD_FIRST)
                            both(i * 2 + (u + 2), a["w_gate"][l], i * CH + (c0 + 1) * CH, i + m, lm, LOAD_SECOND)
                        else:
                            chunk(i * 2 + (u + 1), a["w_up"][l], 0, i * CH + c0 * CH)
                            chunk(i * 2 + (u + 2), a["w_gate"][l], 0, i * CH + (c0 + 1) * CH)
                    both(u + 2 * n - 1, a["w_up"][l], (c0 + n - 1) * CH, m + n - 1, lm, LOAD_ONE if mod_up(l, g) else {})
                    u, m, _ = plan.at[(l, "down", g)]
                    if n == 4:
                        with sp.Fori(0, ND) as i:
                            chunk(i + u, a["w_down"][l], c0 * CH, i * CH)
                    else:
                        for i in range(ND):
                            chunk(u, a["w_down"][l], c0 * CH, i * CH, 2 * n, 2 * n * i)
                if l + 1 < DEPTH:
                    first_unit(plan.at[(l + 1, "win")][0], a["w_in"][l + 1], 0)
                    mod_chunk(plan.at[(l, "mod_pre_mix")][1], l + 1)
            sp.wait_ge(kv_stored, 16 * 4 * DEPTH)
            for n in range(ND):
                for s in range(2):
                    c = slice(n * CH, (n + 1) * CH)
                    sp.wait_ge(x_new, 16 * DEPTH - 8 + 2 * n + s + 1)
                    sp.dma_start(xout[s][:, c], x[:, s, c]).then_inc(x_stored, 16)
            sp.wait_ge(x_stored, 16 * 2 * ND)

        @block.gpsimd
        def _(pool):
            own = [0]

            def link(ins):
                own[0] += 1
                ins.then_inc(pool_own, 1)
                pool.wait_ge(pool_own, own[0])

            def load(dst, src, s):
                pool.dma_start(dst, src).then_inc(s, 16)

            pool.wait_ge(vrows_clear, 1)
            for v, name in enumerate(["norm_mix_pre", "norm_mix_post", "norm_ffn_pre", "norm_ffn_post"]):
                load(vrows[v * 32:v * 32 + 32, 0, :], a[name].rearrange("l (t p) -> (l t) p", p=P), const_loaded)
            for l in range(DEPTH):
                load(vrows[0:96, 1 + l, :], a["mod_b"][l].rearrange("(t p) -> t p", p=P), const_loaded)
            load(vrows[0:16, 3, :], a["c_ctx"].rearrange("(t p) -> t p", p=P), const_loaded)
            load(vrows[16:32, 3, :], a["c"][0].rearrange("(t p) -> t p", p=P), const_loaded)
            load(vrows[32:40, 3, :], a["gmlp_b"].rearrange("l g p -> (l g) p"), const_loaded)
            load(ident[:], a["c_ident"], const_loaded)
            load(rsel[:], a["c_rsel"], const_loaded)
            load(rope[:], a["c_rope"].rearrange("p (a b) -> p a b", a=2), const_loaded)
            load(edge[:], a["c_edge"], const_loaded)
            for s in range(2):
                load(x[:, s, :], xin[s], x_loaded)
            load(rpb_pad, a["c_zero"], pad_cleared)
            pool.wait_ge(pad_cleared, 16)
            load(rpb_pad[:, GRID - 16:GRID + 15].rearrange("(g r) c -> g r c", r=3),
                 a["rpb_a"].rearrange("l h r c -> (l h) r c")[:, 6:9, :], pad_filled)
            pool.wait_ge(pad_filled, 16)
            load(rpb_rows, rpb_pad.unsqueeze(0).broadcast_to([GRID, DEPTH * NH * 3, PADW]), pad_copied)
            pool.wait_ge(pad_copied, 16)

            def power(src, dst, s_in, n_in, s_out):
                pool.wait_ge(s_in, n_in)
                pool.tensor_tensor(dst, src, minus_half[:, 0:dst.shape[-1]], ALU.pow).then_inc(s_out, 1)

            n_rstd = 0
            for l in range(DEPTH):
                n_rstd += 1
                power(ms[:], rstd[:], ms_ready, n_rstd, rstd_ready)
                pool.wait_ge(xt_ready, xt_count(l, 0))
                pool.wait_ge(w_used, (plan.at[(l, "win")][0] + 4) * UNIT)
                load(ck[:, 0:NH, :], a["cache_a_k"][0, l].rearrange("h k d -> k h d"), att_loaded)
                load(ck[:, NH:, :], a["cache_b_k"][0, l].rearrange("h k d -> k h d"), att_loaded)
                load(cv[:, 0:NH, :], a["cache_a_v"][0, l].rearrange("h k d -> k h d"), att_loaded)
                load(cv[:, NH:, :], a["cache_b_v"][0, l].rearrange("h k d -> k h d"), att_loaded)
                load(ln_g[:], a["gmlp_ln_g"][l:l + 1, :].broadcast_to([P, CH]), att_loaded)
                load(ln_b, a["gmlp_ln_b"][l:l + 1, :].broadcast_to([P, CH]), att_loaded)
                load(ws, a["gmlp_w"][l].rearrange("g p q -> p g q"), att_loaded)
                load(sink[:], a["sink_b"][l:l + 1].rearrange("l g r -> l (g r)").broadcast_to([P, NH]), att_loaded)
                for qr in range(2):
                    for kr in range(2):
                        first = (l * NH * 3 + kr - qr + 1) * PADW + GRID - 1
                        src = bass.AP(rpb_rows.tensor, first,
                                      [[DEPTH * NH * 3 * PADW - 1, GRID], [3 * PADW, NH], [1, GRID]])
                        load(bias[qr * GRID:(qr + 1) * GRID, :, kr * GRID:(kr + 1) * GRID], src, att_loaded)
                z_complete(pool, l)
                zb = z[:, 1, Q_B:V_B].rearrange("p (h c) -> p h c", c=P)
                z5 = z[:, 1, Q_B:V_B].rearrange("p (h i c) -> p h i c", i=2, c=32)
                c5 = crossed.rearrange("p h c -> p (h c)").rearrange("p (h i c) -> p h i c", i=2, c=32)
                sn = rope[:, 1, :].rearrange("p (j i c) -> p j i c", j=2, i=2)
                pool.wait_ge(const_loaded, 16 * N_CONST)
                pool.tensor_tensor(turned_b[:], zb, rope[:, 0:1, :].broadcast_to([P, 8, P]), ALU.mult).then_inc(pool_own, 1)
                for i in range(2):
                    for j in range(2):
                        ins = pool.tensor_tensor(c5[:, j::2, i, :], z5[:, j::2, 1 - i, :],
                                                 sn[:, j:j + 1, i, :].broadcast_to([P, 8, 32]), ALU.mult)
                        ins.then_inc(pool_own, 1)
                own[0] += 5
                pool.wait_ge(pool_own, own[0])
                pool.tensor_tensor(turned_b[:], turned_b[:], crossed, ALU.add).then_inc(rope_ready, 1)
                for dst, col, n in ((a["out_2"], K_A, NH), (a["out_3"], V_A, NH), (a["out_4"], K_B, KVB), (a["out_5"], V_B, KVB)):
                    pool.dma_start(dst[0, l].rearrange("h t d -> t h d"),
                                   z[:, 0, col:col + n * P].rearrange("p (h c) -> p h c", c=P)).then_inc(kv_stored, 16)
                for s in range(2):
                    power(vmv[:, s, 1:2], vrstd[:, s:s + 1], vmv_ready, 2 * l + s + 1, vrstd_ready)
                for _ in range(3):
                    n_rstd += 1
                    power(ms[:], rstd[:], ms_ready, n_rstd, rstd_ready)

        @block.tensor
        def _(pe):
            def free(b, i):
                pe.wait_ge(freed[b], i + 1)

            def read(b, i):
                pe.wait_ge(freed[b], i + 2)

            def dense(u, pair, i, hi, lo, nk=KD, ph=0, ready=None, m=None, behind={}):
                free(pair + "0", i)
                free(pair + "1", i)
                for j in range(nk // KB):
                    pe.wait_ge(lo_ready, u * UNIT + (ph + j + 1))
                    slot = (ph + j) % RING
                    for kb in range(KB):
                        k = j * KB + kb
                        if ready:
                            ready(k)
                        mm = products(pair, k, hi, lo, slot, kb, nk)
                    mm.then_inc(w_used, 1)
                    if j in behind:
                        mod(m, behind[j])

            def products(pair, k, hi, lo, slot, kb, nk=KD):
                for s in range(2):
                    t = slice(s * P, (s + 1) * P)
                    for n, (xs, ws_) in enumerate([(lo, whi), (hi, wlo), (hi, whi)]):
                        mm = pe.matmul(bank[f"{pair}{s}"][:], xs[:, k, t], ws_[:, slot, kb, :],
                                       start=(k == 0 and n == 0), stop=(k == nk - 1 and n == 2))
                return mm

            def start():
                half = UNIT // 2
                for m in range(2):
                    mod(m)
                    mod_tail(m)
                turn_x(0, 0, 0)
                for n in range(ND):
                    for i in range(4):
                        m = 2 * (n + 1) + i // 2
                        if n + 1 < ND:
                            mod(m, range(half * (i % 2), half * (i % 2 + 1)))
                            if i == 3:
                                mod_tail(m)
                                turn_x(0, 0, n + 1)
                        q = 4 * n + i
                        _, c, j = start_piece(q)
                        pair = "AB"[c]
                        if j == 0:
                            free(pair + "0", 0)
                            free(pair + "1", 0)
                        pe.wait_ge(xt_ready, 2 * (n + 1))
                        pe.wait_ge(lo_ready, q + 1)
                        for kb in range(KB):
                            mm = products(pair, j * KB + kb, xt_hi, xt_lo, q % RING, kb)
                        mm.then_inc(w_used, 1)
                        if n + 1 < ND and i == 1:
                            mod_tail(m)

            def mod(m, js=range(UNIT)):
                for j in js:
                    pe.wait_ge(mraw_landed[j % RING], m * (16 * UNIT // RING) + 16 * (j // RING + 1))
                    for kb in range(KB):
                        k = j * KB + kb
                        g = 32 * (k % 4)
                        mm = pe.matmul(bank["M"][g:g + 32, :], cond[:, 2 * k:2 * k + 32], mraw[:, j % RING, kb, :],
                                       start=(k < 4), stop=(k >= KD - 4))
                    mm.then_inc(mod_used, 1)

            def mod_tail(i):
                pe.wait_ge(mrow_ready, i + 1)
                free("T", i)
                for t in range(4):
                    mm = pe.matmul(bank["T"][:, 2 * t:2 * t + 2], mrow[:, t * P:(t + 1) * P], rsel[:],
                                   start=True, stop=True)
                mm.then_inc(filled["T"], 1)

            def turn(b, i, tiles):
                free(b, i)
                for n, t in enumerate(tiles):
                    mm = pe.transpose(bank[b][:, n * P:(n + 1) * P], t, ident[:])
                mm.then_inc(filled[b], 1)

            def turn_x(l, which, b):
                for s, (bk, i) in enumerate(plan.at[(l, "pre_uses", which)][b]):
                    pe.wait_ge(xn_ready, 8 * (2 * l + which) + 2 * b + s + 1)
                    turn(bk, i, [f[:, s, (4 * b + t) * P:(4 * b + t + 1) * P] for t in range(4)])

            def pre(l, which):
                def ready(k):
                    if k in (1, 3):
                        turn_x(l, which, 2 + k // 2)
                    if k % 4 == 0:
                        pe.wait_ge(xt_ready, xt_count(l, which) - 8 + 2 * (k // 4 + 1))
                turn_x(l, which, 0)
                turn_x(l, which, 1)
                return ready

            def gates(l, which):
                pe.wait_ge(gate_ready, 2 * l + which + 1)
                for n, uses in enumerate(plan.at[(l, "gate_uses", which)]):
                    for s, (bk, i) in enumerate(uses):
                        turn(bk, i, [gatev[:, 4 * n + t, s:s + 1].broadcast_to([P, P]) for t in range(4)])

            def attention(l):
                got = {}
                for step, banks, m in plan.at[(l, "attention")]:
                    kind = step[0]
                    if kind in ("mod_first", "mod_second"):
                        mod(m, range(UNIT // 2) if kind == "mod_first" else range(UNIT // 2, UNIT))
                    elif kind == "mod_tail":
                        mod_tail(m)
                    elif kind == "turn":
                        s, b = step[1:]
                        if s == b == 0:
                            z_complete(pe, l)
                        if s == 1 and b == 3:
                            pe.wait_ge(rope_ready, l + 1)
                        turn(*banks[0], [z[:, s, h * P:(h + 1) * P] if h < 12 else
                                         turned_b[:, h - 12, :] if s else z[:, 0, Q_B + (h - 12) * P:Q_B + (h - 11) * P]
                                         for h in range(4 * b, 4 * b + 4)])
                    elif kind == "turn_ck":
                        b = step[1]
                        pe.wait_ge(att_loaded, 16 * N_ATT * (l + 1))
                        turn(*banks[0], [ck[:, h, :] for h in range(4 * b, 4 * b + 4)])
                    elif kind == "turn_ws":
                        pe.wait_ge(att_loaded, 16 * N_ATT * (l + 1))
                        turn(*banks[0], [ws[:, g, :] for g in range(GC)])
                    elif kind == "score":
                        n = step[1]
                        s, ty = divmod(n, 2)
                        for b, i in [got[("turn", s, j)][0] for j in range(5)] + [got[("turn_ck", j)][0] for j in range(2 * s)]:
                            read(b, i)
                        for (b, i), heads in zip(banks, score_banks(n)):
                            free(b, i)
                            for j, h in enumerate(heads):
                                q, k, c = (h, 6 + h, h) if ty == 0 else (12 + h, 18 + h // 3, 6 + h // 3)
                                o = j * P * (1 + s)
                                mm = pe.matmul(bank[b][:, o:o + P], qkt[:, q, :], qkt[:, k, :], start=True, stop=True)
                                if s:
                                    mm = pe.matmul(bank[b][:, o + P:o + 2 * P], qkt[:, q, :], ckt[:, c, :],
                                                   start=True, stop=True)
                            mm.then_inc(filled[b], 1)
                    elif kind == "value":
                        n = step[1]
                        s, ty = divmod(n, 2)
                        pe.wait_ge(pn_ready, 4 * l + n + 1)
                        blocks = [prob[:, n % 2, h, w * P:(w + 1) * P] for h in range(NH) for w in range(1 + s)]
                        turns, outs = banks[:-2], banks[-2:]
                        for j, (b, i) in enumerate(turns):
                            turn(b, i, blocks[4 * j:4 * j + 4])
                        for b, i in turns:
                            read(b, i)
                        for (b, i), heads in zip(outs, (range(0, 4), range(4, 6))):
                            free(b, i)
                            for j, h in enumerate(heads):
                                kv = h if ty == 0 else 6 + h // 3
                                col = V_A + h * P if ty == 0 else V_B + (h // 3) * P
                                vs = [z[:, s, col:col + P]] + s * [cv[:, kv, :]]
                                for w, v in enumerate(vs):
                                    mm = pe.matmul(bank[b][:, j * P:(j + 1) * P], v, pt[:, h * (1 + s) + w, :],
                                                   start=(w == 0), stop=(w == s))
                            mm.then_inc(filled[b], 1)
                    elif kind == "gate_c":
                        s = step[1]
                        pe.wait_ge(vn_ready, 2 * l + s + 1)
                        read(*got[("turn_ws",)][0])
                        b, i = banks[0]
                        free(b, i)
                        for g in range(GC):
                            mm = pe.matmul(bank[b][:, g * P:(g + 1) * P], wst[:, g, :],
                                           z[:, s, V_C + g * P:V_C + (g + 1) * P], start=True, stop=True)
                        mm.then_inc(filled[b], 1)
                    elif kind == "turn_c":
                        s = step[1]
                        read(*got[("gate_c", s)][0])
                        turn(*banks[0], [z[:, s, U_C + g * P:U_C + (g + 1) * P] for g in range(GC)])
                    if banks:
                        got[step] = banks
                return got

            pe.wait_ge(const_loaded, 16 * N_CONST)
            pe.wait_ge(freed["X0"], 1)
            for t in range(4):
                mm = pe.transpose(bank["X0"][:, t * P:(t + 1) * P], vrows[:, t, :], ident[:])
            mm.then_inc(filled["X0"], 1)
            pe.wait_ge(cond_ready, 1)
            start()
            for l in range(DEPTH):
                u, m, use = plan.at[(l, "win")]
                if l == 0:
                    m -= 1

                def pair(i, ready=None):
                    dense(i * 2 + u, "A", i + use["A0"], xt_hi, xt_lo, ready=ready, m=i + m, behind=IN_FIRST)
                    dense(i * 2 + (u + 1), "B", i + use["B0"], xt_hi, xt_lo, m=i + m, behind=IN_SECOND)
                    mod_tail(i + m)

                if l:
                    pair(0, pre(l, 0))
                with pe.Fori(1, W_INC // 2) as i:
                    pair(i)
                dense(u + W_INC - 1, "A", use["A0"] + W_INC // 2, xt_hi, xt_lo, m=m + W_INC // 2,
                      behind={} if l else IN_ONE)
                if l == 0:
                    mod_tail(m + W_INC // 2)
                got = attention(l)
                gates(l, 0)
                u, m, use = plan.at[(l, "out")]
                for step, banks in got.items():
                    if step[0] in ("value", "turn_c"):
                        for b, i in banks[-2:]:
                            read(b, i)
                with pe.Fori(0, ND // 2) as i:
                    dense(i * 2 + u, "A", i + use["A0"], xt_hi, xt_lo, m=i + m, behind=IN_FIRST)
                    dense(i * 2 + (u + 1), "B", i + use["B0"], xt_hi, xt_lo, m=i + m, behind=IN_SECOND)
                    mod_tail(i + m)
                mod(m + MOD_OUT)
                mod_tail(m + MOD_OUT)
                ready = pre(l, 1)
                for g, (c0, n) in enumerate(GROUPS):
                    u, m, use = plan.at[(l, "up", g)]

                    def turn_hidden(i):
                        for s in range(2):
                            read(f"B{s}", i + use[f"B{s}"])
                            turn(f"X{s}", i + use[f"X{s}"], [hid[:, s, t * P:(t + 1) * P] for t in range(4)])

                    dense(u, "A", use["A0"], xt_hi, xt_lo, ready=None if g else ready)
                    first, second, one = (IN_FIRST, IN_SECOND, IN_ONE) if mod_up(l, g) else ({}, {}, {})
                    with pe.Fori(0, n - 1) as i:
                        dense(i * 2 + (u + 1), "B", i + use["B0"], xt_hi, xt_lo, m=i + m, behind=first)
                        dense(i * 2 + (u + 2), "A", i + (use["A0"] + 1), xt_hi, xt_lo, m=i + m, behind=second)
                        turn_hidden(i)
                        if mod_up(l, g):
                            mod_tail(i + m)
                    dense(u + 2 * n - 1, "B", use["B0"] + n - 1, xt_hi, xt_lo, m=m + n - 1, behind=one)
                    if mod_up(l, g):
                        mod_tail(m + n - 1)

                    def hidden_first(k):
                        if k == KB:
                            turn_hidden(n - 1)
                            if g == 1:
                                gates(l, 1)
                        hidden_ready(k)

                    def hidden_ready(k):
                        if k % 4 == 0:
                            for s in range(2):
                                read(f"X{s}", use[f"X{s}"] + k // 4)

                    u, m, use2 = plan.at[(l, "down", g)]
                    for i in range(ND):
                        p = "AB"[i % 2]
                        dense(u, p, use2[p + "0"] + i // 2, ht_hi, ht_lo, nk=4 * n, ph=2 * n * i,
                              ready=hidden_ready if i else hidden_first)
                if l + 1 < DEPTH:
                    _, m, _ = plan.at[(l, "mod_pre_mix")]
                    mod(m)
                    mod_tail(m)

        def ahead(split, u, ph=0, pieces=UNIT, between=None, leave=0):
            for j in range(pieces - leave):
                split(u, ph + LEAD + j)
                if between and j == pieces - 1 - max(leave, 1):
                    between()

        def left_over(split, u, ph=0, pieces=UNIT, part=None):
            for j in range(LEFT) if part is None else [part]:
                split(u, ph + LEAD + pieces - LEFT + j)

        def past_end(u, ph):
            return isinstance(u, int) and u * UNIT + ph >= TOTAL

        @block.scalar
        def _(act):
            n_sq = [0]
            n_hi = [0]

            def split(u, ph):
                if past_end(u, ph):
                    return
                act.wait_ge(raw_landed[ph % RING], u * (16 * UNIT // RING) + 16 * (ph // RING + 1))
                if not (isinstance(u, int) and u * UNIT + ph < RING):
                    act.wait_ge(w_used, u * UNIT + (ph - RING + 1))
                act.copy(whi[:, ph % RING], raw[:, ph % RING]).then_inc(hi_ready, 1)

            def fill_of(b, i):
                act.wait_ge(filled[b], plan.fill.get((b, i), i + 1) if isinstance(i, int) else i + 1)

            def square(src, dst):
                if n_sq[0]:
                    act.wait_ge(sq_ready, n_sq[0])
                n_sq[0] += 1
                act.activation(junk[:], src, ACT.Square, accum_out=dst).then_inc(sq_ready, 1)

            def high(dst, src):
                n_hi[0] += 1
                act.copy(dst, src).then_inc(hi_x, 1)

            def mod_row(i):
                act.wait_ge(mod_used, i * UNIT + UNIT)
                if not (isinstance(i, int) and i == 0):
                    act.wait_ge(filled["T"], i)
                act.copy(mrow[:], bank["M"][:]).then_inc(mrow_ready, 1)

            def squares(l, which, m=None):
                for n in range(ND):
                    if m and n == ND - 1:
                        mod_row(m)
                    for s in range(2):
                        if l or which:
                            act.wait_ge(x_new, 16 * l - 8 * (1 - which) + 2 * n + s + 1)
                        square(x[:, s, n * CH:(n + 1) * CH], ssx[:, s, n:n + 1])

            def pre_part(l, which, b):
                uses = plan.at[(l, "pre_uses", which)][b]
                bk, i = uses[1]
                fill_of(bk, i)
                if b > 1:
                    act.wait_ge(xt_ready, xt_count(l, which) - 8 + 2 * (b - 1))
                for t in range(4):
                    k = 4 * b + t
                    ins = act.activation(xtmp[:, b % 2, 1, t, :], bank[bk][:, t * P:(t + 1) * P], ACT.Identity,
                                         scale=scal[:, k, 1:2], bias=shift[:, k, 1:2])
                ins.then_inc(freed[bk], 1)
                for s, (bk, i) in enumerate(uses):
                    act.wait_ge(freed[bk], i + 2)
                    high(xt_hi[:, 4 * b:4 * b + 4, s * P:(s + 1) * P], xtmp[:, b % 2, s])

            def pre(l, which, m=None):
                squares(l, which, m)
                act.wait_ge(vec_ready, vec_count(l, which))
                for b in range(ND):
                    pre_part(l, which, b)

            def start():
                for m in range(2):
                    mod_row(m)
                act.wait_ge(vec_ready, 1)
                pre_part(0, 0, 0)
                for n in range(ND):
                    for i in range(4):
                        if i % 2 and n + 1 < ND:
                            mod_row(2 * (n + 1) + i // 2)
                            if i == 3:
                                act.wait_ge(vec_ready, n + 2)
                                pre_part(0, 0, n + 1)
                        split(0, 4 * n + i + LEAD)

            def gates(l, which):
                if which == 0:
                    act.wait_ge(kv_stored, 16 * 4 * (l + 1))
                for n, uses in enumerate(plan.at[(l, "gate_uses", which)]):
                    bk, i = uses[0]
                    fill_of(bk, i)
                    act.copy(gate[:, 0, n * CH:(n + 1) * CH], bank[bk][:]).then_inc(freed[bk], 1)

            def attention(l):
                z_complete(act, l)
                for step, banks, m in plan.at[(l, "attention")]:
                    kind = step[0]
                    if step in GELU_BEFORE:
                        s = GELU_BEFORE.index(step)
                        act.activation(z[:, s, U_C:W_IN], z[:, s, U_C:W_IN], ACT.Gelu_apprx_tanh).then_inc(gelu_ready, 1)
                    if kind == "mod_second":
                        mod_row(m)
                    elif kind in ("turn", "turn_ck", "turn_ws"):
                        b, i = banks[0]
                        dst = {"turn": qkt, "turn_ck": ckt, "turn_ws": wst}[kind]
                        j = step[-1] if kind != "turn_ws" else 0
                        if b == "X0":
                            fill_of(b, i)
                            act.copy(dst[:, 4 * j:4 * j + 4, :], four(bank[b][:])).then_inc(freed[b], 1)
                    elif kind == "score":
                        n = step[1]
                        s, ty = divmod(n, 2)
                        w = P * (1 + s)
                        act.wait_ge(nm_ready, 4 * l + n + 1)
                        for (b, i), heads in zip(banks, score_banks(n)):
                            for j, h in enumerate(heads):
                                dst = prob[:, n % 2, h, 0:w]
                                src = dst if n == 2 else bank[b][:, j * w:(j + 1) * w]
                                ins = act.activation(dst, src, ACT.Exp, bias=nmax[:, n, h:h + 1],
                                                     scale=1.0 if n == 2 else SCALE, accum_out=den[:, n, h:h + 1])
                            if n != 2:
                                ins.then_inc(freed[b], 1)
                        if ty:
                            ins = act.activation(esink[:, n, :], esink[:, n, :], ACT.Exp)
                        ins.then_inc(exp_ready, 1) if ty or n == 2 else exp_last(n)
                    elif kind == "value":
                        n = step[1]
                        s, ty = divmod(n, 2)
                        for j, (b, i) in enumerate(banks[:-2]):
                            if b == "X0":
                                fill_of(b, i)
                                k = min(4, NH * (1 + s) - 4 * j)
                                act.copy(pt[:, 4 * j:4 * j + k, :], four(bank[b][:])[:, 0:k, :]).then_inc(freed[b], 1)
                        for (b, i), heads in zip(banks[-2:], (range(0, 4), range(4, 6))):
                            fill_of(b, i)
                            k = len(heads)
                            k0 = ty * NH + heads[0]
                            high(xt_hi[:, k0:k0 + k, s * P:(s + 1) * P], four(bank[b][:])[:, 0:k, :])
                    elif kind == "turn_c":
                        s = step[1]
                        b, i = banks[0]
                        fill_of(b, i)
                        high(xt_hi[:, 12:16, s * P:(s + 1) * P], four(bank[b][:]))

            def exp_last(n):
                act.activation(esink[:, n, 0:1], nmax[:, n, 0:1], ACT.Copy).then_inc(exp_ready, 1)

            act.wait_ge(freed["X0"], 2)
            act.activation(silu_c[:].rearrange("p c t -> p (c t)"), vcols[:, 3 * P:3 * P + 2 * KD],
                           ACT.Silu).then_inc(silu_ready, 1)
            for j in range(LEAD):
                split(0, j)
            act.wait_ge(x_loaded, 32)
            squares(0, 0)
            start()
            for l in range(DEPTH):
                u, m, _ = plan.at[(l, "win")]
                if l:
                    pre(l, 0, plan.at[(l - 1, "mod_pre_mix")][1])
                    ahead(split, u)
                    ahead(split, u + 1, between=lambda: mod_row(m))
                else:
                    m -= 1
                with act.Fori(1, W_INC // 2) as i:
                    ahead(split, i * 2 + u)
                    ahead(split, i * 2 + (u + 1), between=lambda: mod_row(i + m))
                ahead(split, u + W_INC - 1, between=None if l else lambda: mod_row(m + W_INC // 2))
                attention(l)
                gates(l, 0)
                u, m, use = plan.at[(l, "out")]
                for i in range(ND):
                    ahead(split, u + i, between=(lambda: mod_row(m + i // 2)) if i % 2 else None,
                          leave=LEFT if i == ND - 1 else 0)
                    act.wait_ge(w_used, (u + i + 1) * UNIT)
                    b = f"{'AB'[i % 2]}0"
                    act.copy(f[:, 0, i * CH:(i + 1) * CH], bank[b][:]).then_inc(freed[b], 1)
                    for s in range(2):
                        b = f"{'AB'[i % 2]}{s}"
                        act.wait_ge(freed[b], use[b] + i // 2 + 2)
                        square(f[:, s, i * CH:(i + 1) * CH], ssq[:, s, i:i + 1])
                left_over(split, u + ND - 1)
                pre(l, 1, m + MOD_OUT)
                for g, (c0, n) in enumerate(GROUPS):
                    u, m, use = plan.at[(l, "up", g)]

                    def silu(u, i, first=False):
                        act.wait_ge(w_used, u * UNIT + UNIT)
                        if not (first and g == 0 and l == 0):
                            act.wait_ge(freed["B1"], i + (use["B1"] + 1))
                        for s in range(2):
                            act.activation(sil[:, s, :], bank[f"A{s}"][:], ACT.Silu).then_inc(freed[f"A{s}"], 1)

                    def hidden_high(i):
                        for s in range(2):
                            act.wait_ge(filled[f"X{s}"], i + (use[f"X{s}"] + 1))
                            act.wait_ge(x_loaded, 32)
                            act.copy(ht_hi[:, bass.ds(i * 4, 4), s * P:(s + 1) * P],
                                     four(bank[f"X{s}"][:])).then_inc(ht_hi_ready, 1)

                    ahead(split, u)
                    silu(u, 0, True)
                    with act.Fori(0, n - 1) as i:
                        ahead(split, i * 2 + (u + 1))
                        ahead(split, i * 2 + (u + 2), between=(lambda: mod_row(i + m)) if mod_up(l, g) else None)
                        silu(i * 2 + (u + 2), i + 1)
                        hidden_high(i)
                    ahead(split, u + 2 * n - 1, between=(lambda: mod_row(m + n - 1)) if mod_up(l, g) else None)
                    hidden_high(n - 1)
                    if g == 1:
                        gates(l, 1)
                    u, m, use2 = plan.at[(l, "down", g)]
                    for i in range(ND):
                        if n == 4:
                            ahead(split, u + i)
                            act.wait_ge(w_used, (u + i + 1) * UNIT)
                        else:
                            ahead(split, u, 2 * n * i, 2 * n, leave=LEFT if i == ND - 1 else 0)
                            act.wait_ge(w_used, u * UNIT + 2 * n * (i + 1))
                        for s in range(2):
                            b = f"{'AB'[i % 2]}{s}"
                            if g == 0:
                                act.copy(f[:, s, i * CH:(i + 1) * CH], bank[b][:]).then_inc(freed[b], 1)
                            elif g == 2:
                                act.wait_ge(freed[b], use2[b] + i // 2 + 2)
                                square(f[:, s, i * CH:(i + 1) * CH], ssq[:, s, i:i + 1])
                    if g == len(GROUPS) - 1:
                        left_over(split, u, 2 * n * (ND - 1), 2 * n)

        @block.vector
        def _(dve):
            own = [0]
            n_hi = [0]

            def link(ins):
                own[0] += 1
                ins.then_inc(dve_own, 1)
                dve.wait_ge(dve_own, own[0])

            def split(u, ph):
                if past_end(u, ph):
                    return
                dve.wait_ge(hi_ready, u * UNIT + (ph + 1))
                if not (isinstance(u, int) and u * UNIT + ph < RING):
                    dve.wait_ge(w_used, u * UNIT + (ph - RING + 1))
                dve.tensor_tensor(wlo[:, ph % RING], raw[:, ph % RING], whi[:, ph % RING].bitcast(F32),
                                  ALU.subtract).then_inc(lo_ready, 1)

            def fill_of(b, i):
                dve.wait_ge(filled[b], plan.fill.get((b, i), i + 1) if isinstance(i, int) else i + 1)

            def mod_cols(i, col=None):
                dve.wait_ge(filled["T"], i + 1)
                dve.tensor_scalar(modt[:, bass.ds((i if col is None else col) * 8, 8)], bank["T"][:, 0:8], 1.0, None, ALU.mult).then_inc(freed["T"], 1)

            def mean_square(sums, j, meanwhile=None):
                dve.wait_ge(sq_ready, 8 * j)
                link(dve.tensor_reduce(msum[:], sums, AX_X, ALU.add))
                dve.tensor_scalar(ms[:], msum[:], 1.0 / D, EPS, ALU.mult, ALU.add).then_inc(ms_ready, 1)
                if meanwhile:
                    meanwhile()
                dve.wait_ge(rstd_ready, j)

            def low(dst, src, hi, s_out):
                n_hi[0] += 1
                dve.wait_ge(hi_x, n_hi[0])
                dve.tensor_tensor(dst, src, hi.bitcast(F32), ALU.subtract).then_inc(s_out, 1)

            def norm_vectors(l, which, ks=slice(0, KD), m=None):
                v = 3 * which
                dve.wait_ge(freed["T"], (m or mod_done(l, v + 1)) + 1)
                link(dve.tensor_tensor(scal[:, ks], mod_t(l, v + 1)[:, ks], mod_b(l, v + 1)[:, ks], ALU.add))
                dve.tensor_tensor(shift[:, ks], mod_t(l, v)[:, ks], mod_b(l, v)[:, ks], ALU.add)
                dve.scalar_tensor_tensor(out=scal[:, ks], in0=scal[:, ks], scalar=1.0, in1=vec(2 * which, l)[:, ks],
                                         op0=ALU.add, op1=ALU.mult).then_inc(vec_ready, 1)

            def normalise(l, which, meanwhile=None):
                mean_square(ssx[:], 4 * l + 2 * which + 1, meanwhile)
                normal_chunks(range(ND // 2))

            def normal_chunks(ns):
                for n in ns:
                    c = slice(n * CH, (n + 1) * CH)
                    for s in range(2):
                        dve.tensor_scalar(f[:, s, c], x[:, s, c], rstd[:, s:s + 1], None, ALU.mult).then_inc(xn_ready, 1)

            def pre_part(l, which, b):
                bk, i = plan.at[(l, "pre_uses", which)][b][0]
                fill_of(bk, i)
                if b > 1:
                    dve.wait_ge(xt_ready, xt_count(l, which) - 8 + 2 * (b - 1))
                for t in range(4):
                    k = 4 * b + t
                    ins = dve.tensor_scalar(xtmp[:, b % 2, 0, t, :], bank[bk][:, t * P:(t + 1) * P], scal[:, k, 0:1],
                                            shift[:, k, 0:1], ALU.mult, ALU.add)
                ins.then_inc(freed[bk], 1)
                for s in range(2):
                    t = (slice(None), slice(4 * b, 4 * b + 4), slice(s * P, (s + 1) * P))
                    low(xt_lo[t], xtmp[:, b % 2, s], xt_hi[t], xt_ready)
                if b == 0:
                    normal_chunks(range(ND // 2, ND))

            def pre(l, which, after_first=None):
                dve.wait_ge(vec_ready, vec_count(l, which))
                for b in range(ND):
                    pre_part(l, which, b)
                    if after_first and b == 0:
                        after_first()

            def start():
                def part(n):
                    norm_vectors(0, 0, slice(4 * n, 4 * n + 4), 2 * (n + 1))
                    dve.wait_ge(vec_ready, n + 1)
                    pre_part(0, 0, n)

                for m in range(2):
                    mod_cols(m, start_chunk(m))
                part(0)
                for n in range(ND):
                    for i in range(4):
                        m = 2 * (n + 1) + i // 2
                        if i == 3 and n + 1 < ND:
                            mod_cols(m, start_chunk(m))
                            part(n + 1)
                        split(0, 4 * n + i + LEAD)
                        if i == 1 and n + 1 < ND:
                            mod_cols(m, start_chunk(m))
                        elif i == 1:
                            read_out(0, 0, "A", 2 * UNIT - 2)
                read_out(1, CH, "B")

            def read_out(u, col, pair, used=None):
                dve.wait_ge(w_used, used or u * UNIT + UNIT)
                for s in range(2):
                    dve.tensor_scalar(z[:, s, bass.ds(col, CH)], bank[f"{pair}{s}"][:], 1.0, None,
                                      ALU.mult).then_inc(freed[f"{pair}{s}"], 1)

            def gate_vector(l, which):
                v = 3 * which + 2
                dve.wait_ge(freed["T"], mod_done(l, v) + 1)
                link(dve.tensor_tensor(gatev[:], mod_t(l, v), mod_b(l, v), ALU.add))
                dve.tensor_tensor(gatev[:], gatev[:], vec(2 * which + 1, l), ALU.mult).then_inc(gate_ready, 1)

            def gates(l, which):
                if which == 0:
                    dve.wait_ge(kv_stored, 16 * 4 * (l + 1))
                for n, uses in enumerate(plan.at[(l, "gate_uses", which)]):
                    bk, i = uses[1]
                    fill_of(bk, i)
                    dve.tensor_copy(gate[:, 1, n * CH:(n + 1) * CH], bank[bk][:]).then_inc(freed[bk], 1)

            def post(l, which, meanwhile=None):
                mean_square(ssq[:], 4 * l + 2 * which + 2, meanwhile)
                for n in range(ND):
                    c = slice(n * CH, (n + 1) * CH)
                    for s in range(2):
                        dve.scalar_tensor_tensor(out=x[:, s, c], in0=f[:, s, c], scalar=rstd[:, s:s + 1], in1=x[:, s, c],
                                                 op0=ALU.mult, op1=ALU.add).then_inc(x_new, 1)

            def gated(l, which, n):
                for s in range(2):
                    bk, i = plan.at[(l, "gate_uses", which)][n][s]
                    dve.wait_ge(freed[bk], i + 2)
                    dve.wait_ge(sq_ready, 8 * (4 * l + 2 * which + 1) + 2 * n + s + 1)
                    c = slice(n * CH, (n + 1) * CH)
                    ins = dve.tensor_tensor(f[:, s, c], f[:, s, c], gate[:, s, c], ALU.mult)
                link(ins)

            def attention(l):
                dve.wait_ge(att_loaded, 16 * N_ATT * (l + 1))
                dve.tensor_tensor(bias[:], bias[:], edge[:].unsqueeze(1).broadcast_to([P, NH, P]), ALU.add)
                link(dve.tensor_scalar(nsink[:], sink[:], -1.0, None, ALU.mult))
                for step, banks, m in plan.at[(l, "attention")]:
                    kind = step[0]
                    if kind == "mod_tail":
                        mod_cols(m)
                    elif kind in ("turn", "turn_ck", "turn_ws"):
                        b, i = banks[0]
                        dst = {"turn": qkt, "turn_ck": ckt, "turn_ws": wst}[kind]
                        j = step[-1] if kind != "turn_ws" else 0
                        if b == "X1":
                            fill_of(b, i)
                            dve.tensor_copy(dst[:, 4 * j:4 * j + 4, :], four(bank[b][:])).then_inc(freed[b], 1)
                    elif kind == "score":
                        n = step[1]
                        s, ty = divmod(n, 2)
                        w = P * (1 + s)
                        for (b, i), heads in zip(banks, score_banks(n)):
                            fill_of(b, i)
                            k = len(heads)
                            sc = bank[b][:, 0:k * w].rearrange("p (h w) -> p h w", w=w)
                            hs = slice(heads[0], heads[0] + k)
                            if n == 2:
                                dve.scalar_tensor_tensor(out=prob[:, 0, hs, 0:P], in0=sc[:, :, 0:P], scalar=SCALE,
                                                         in1=bias[:, hs, :], op0=ALU.mult, op1=ALU.add)
                                ins = dve.tensor_scalar(prob[:, 0, hs, P:w], sc[:, :, P:w], SCALE, None, ALU.mult)
                                ins.then_inc(freed[b], 1)
                            else:
                                ins = dve.tensor_reduce(rmax[:, n, hs], sc, AX_X, ALU.max)
                        if n == 2:
                            dve.wait_ge(freed[b], i + 2)
                            ins = dve.tensor_reduce(rmax[:, n, :], prob[:, 0, :, :], AX_X, ALU.max)
                        link(ins)
                        if ty:
                            link(dve.scalar_tensor_tensor(out=nmax[:, n, :], in0=rmax[:, n, :], scalar=-SCALE,
                                                          in1=nsink[:], op0=ALU.mult, op1=ALU.min))
                            dve.tensor_tensor(esink[:, n, :], nmax[:, n, :], sink[:], ALU.add).then_inc(nm_ready, 1)
                        else:
                            dve.tensor_scalar(nmax[:, n, :], rmax[:, n, :], -1.0 if n == 2 else -SCALE, None,
                                              ALU.mult).then_inc(nm_ready, 1)
                    elif kind == "soft":
                        n = step[1]
                        s, ty = divmod(n, 2)
                        w = P * (1 + s)
                        dve.wait_ge(exp_ready, 4 * l + n + 1)
                        if ty:
                            link(dve.tensor_tensor(den[:, n, :], den[:, n, :], esink[:, n, :], ALU.add))
                        link(dve.reciprocal(den[:, n, :], den[:, n, :]))
                        pr = prob[:, n % 2, :, 0:w]
                        dve.tensor_tensor(pr, pr, den[:, n, :].unsqueeze(2).broadcast_to([P, NH, w]),
                                          ALU.mult).then_inc(pn_ready, 1)
                    elif kind == "value":
                        n = step[1]
                        s, ty = divmod(n, 2)
                        for j, (b, i) in enumerate(banks[:-2]):
                            if b == "X1":
                                fill_of(b, i)
                                k = min(4, NH * (1 + s) - 4 * j)
                                dve.tensor_copy(pt[:, 4 * j:4 * j + k, :], four(bank[b][:])[:, 0:k, :]).then_inc(freed[b], 1)
                        for (b, i), heads in zip(banks[-2:], (range(0, 4), range(4, 6))):
                            k = len(heads)
                            k0 = ty * NH + heads[0]
                            t = (slice(None), slice(k0, k0 + k), slice(s * P, (s + 1) * P))
                            low(xt_lo[t], four(bank[b][:])[:, 0:k, :], xt_hi[t], freed[b])
                    elif kind == "norm_v":
                        s = step[1]
                        v = z[:, s, V_C:W_IN]
                        dve.wait_ge(gelu_ready, 2 * l + s + 1)
                        link(dve.bn_stats(vstat[:, s, :], v))
                        link(dve.bn_aggr(vmv[:, s, :], vstat[:, s, :]))
                        dve.tensor_scalar(vmv[:, s, 1:2], vmv[:, s, 1:2], EPS, None, ALU.add).then_inc(vmv_ready, 1)
                        dve.wait_ge(vrstd_ready, 2 * l + s + 1)
                        link(dve.tensor_scalar(v, v, vmv[:, s, 0:1], vrstd[:, s:s + 1], ALU.subtract, ALU.mult))
                        link(dve.tensor_tensor(v, v, ln_g[:], ALU.mult))
                        dve.tensor_tensor(v, v, ln_b, ALU.add).then_inc(vn_ready, 1)
                    elif kind == "gate_c":
                        s = step[1]
                        b, i = banks[0]
                        fill_of(b, i)
                        for g in range(GC):
                            ug = z[:, s, U_C + g * P:U_C + (g + 1) * P]
                            c = 3 * P + 2 * KD + l * GC + g
                            ins = dve.scalar_tensor_tensor(out=ug, in0=bank[b][:, g * P:(g + 1) * P],
                                                           scalar=vcols[:, c:c + 1], in1=ug, op0=ALU.add, op1=ALU.mult)
                        ins.then_inc(freed[b], 1)
                    elif kind == "turn_c":
                        s = step[1]
                        b, i = banks[0]
                        t = (slice(None), slice(12, 16), slice(s * P, (s + 1) * P))
                        low(xt_lo[t], four(bank[b][:]), xt_hi[t], freed[b])

            dve.memset(vrows, 0.0).then_inc(vrows_clear, 1)
            dve.memset(minus_half[:], -0.5)
            dve.memset(cond[:, 2 * KD:], 0.0)
            for b in BANKS:
                dve.memset(clear[:, BANKS.index(b):BANKS.index(b) + 1], 0.0).then_inc(freed[b], 1)
            fill_of("X0", 0)
            dve.tensor_copy(vcols[:], bank["X0"][:]).then_inc(freed["X0"], 1)
            dve.wait_ge(silu_ready, 1)
            dve.tensor_copy(cond[:, 0:2 * KD].rearrange("p (t c) -> p t c", c=2),
                            silu_c[:].rearrange("p c t -> p t c")).then_inc(cond_ready, 1)
            for j in range(LEAD):
                split(0, j)
            normalise(0, 0)
            start()
            for l in range(DEPTH):
                if l:
                    pre(l, 0, lambda: left_over(split, u, 2 * n * (ND - 1), 2 * n, 1))
                u, m, use = plan.at[(l, "win")]

                def pair(i):
                    ahead(split, i * 2 + u)
                    read_out(i * 2 + u, i * 2 * CH, "A")
                    ahead(split, i * 2 + (u + 1))
                    read_out(i * 2 + (u + 1), i * 2 * CH + CH, "B")
                    mod_cols(i + m)

                if l:
                    pair(0)
                else:
                    m -= 1
                with dve.Fori(1, W_INC // 2) as i:
                    pair(i)
                ahead(split, u + W_INC - 1)
                read_out(u + W_INC - 1, (W_INC - 1) * CH, "A")
                if l == 0:
                    mod_cols(m + W_INC // 2)
                gate_vector(l, 0)
                attention(l)
                gates(l, 0)
                u, m, use = plan.at[(l, "out")]
                for i in range(ND):
                    ahead(split, u + i, leave=LEFT if i == ND - 1 else 0)
                    dve.wait_ge(w_used, (u + i + 1) * UNIT)
                    b = f"{'AB'[i % 2]}1"
                    dve.tensor_copy(f[:, 1, i * CH:(i + 1) * CH], bank[b][:]).then_inc(freed[b], 1)
                    if i % 2:
                        mod_cols(m + i // 2)
                    gated(l, 0, i)
                post(l, 0, lambda: left_over(split, u + ND - 1, part=0))

                def last_mod():
                    mod_cols(m + MOD_OUT)
                    norm_vectors(l, 1)

                normalise(l, 1, last_mod)
                pre(l, 1, lambda: left_over(split, u + ND - 1, part=1))
                for g, (c0, n) in enumerate(GROUPS):
                    u, m, use = plan.at[(l, "up", g)]

                    def multiply(u, i):
                        dve.wait_ge(w_used, u * UNIT + UNIT)
                        dve.wait_ge(filled["X1"], i + use["X1"])
                        for s in range(2):
                            dve.wait_ge(freed[f"A{s}"], i + (use[f"A{s}"] + 2))
                            dve.tensor_tensor(hid[:, s, :], sil[:, s, :], bank[f"B{s}"][:],
                                              ALU.mult).then_inc(freed[f"B{s}"], 1)

                    def hidden_low(i, first):
                        for s in range(2):
                            dve.wait_ge(ht_hi_ready, i * 2 + (first + s + 1))
                            t = (slice(None), bass.ds(i * 4, 4), slice(s * P, (s + 1) * P))
                            dve.tensor_tensor(ht_lo[t], four(bank[f"X{s}"][:]), ht_hi[t].bitcast(F32),
                                              ALU.subtract).then_inc(freed[f"X{s}"], 1)

                    first = 2 * (FFC * l + c0)
                    ahead(split, u)
                    with dve.Fori(0, n - 1) as i:
                        ahead(split, i * 2 + (u + 1))
                        multiply(i * 2 + (u + 1), i)
                        ahead(split, i * 2 + (u + 2))
                        hidden_low(i, first)
                        if mod_up(l, g):
                            mod_cols(i + m)
                    ahead(split, u + 2 * n - 1)
                    multiply(u + 2 * n - 1, n - 1)
                    hidden_low(n - 1, first)
                    if mod_up(l, g):
                        mod_cols(m + n - 1)
                    if g == 0:
                        gate_vector(l, 1)
                    if g == 1:
                        gates(l, 1)
                    u, m, use2 = plan.at[(l, "down", g)]
                    for i in range(ND):
                        if n == 4:
                            ahead(split, u + i)
                            dve.wait_ge(w_used, (u + i + 1) * UNIT)
                        else:
                            ahead(split, u, 2 * n * i, 2 * n, leave=LEFT if i == ND - 1 else 0)
                            dve.wait_ge(w_used, u * UNIT + 2 * n * (i + 1))
                        for s in range(2):
                            b = f"{'AB'[i % 2]}{s}"
                            if g:
                                c = slice(i * CH, (i + 1) * CH)
                                dve.tensor_tensor(f[:, s, c], f[:, s, c], bank[b][:], ALU.add).then_inc(freed[b], 1)
                        if g == len(GROUPS) - 1:
                            gated(l, 1, i)
                post(l, 1, lambda: left_over(split, u, 2 * n * (ND - 1), 2 * n, 0))

                def last_mod():
                    mod_cols(plan.at[(l, "mod_pre_mix")][1])
                    norm_vectors(l + 1, 0)

                if l + 1 < DEPTH:
                    normalise(l + 1, 0, last_mod)



_INS = ['x_prompt', 'x_sample', 'cache_a_k', 'cache_a_v', 'cache_b_k', 'cache_b_v', 'c', 'c_ctx', 'mod_w', 'mod_b',
        'norm_mix_pre', 'norm_mix_post', 'norm_ffn_pre', 'norm_ffn_post', 'w_in', 'w_out', 'rpb_a', 'sink_b',
        'gmlp_ln_g', 'gmlp_ln_b', 'gmlp_w', 'gmlp_b', 'w_gate', 'w_up', 'w_down']
_OUTS = [(1, 128, 2048), (1, 128, 2048), (1, 2, 6, 128, 128), (1, 2, 6, 128, 128), (1, 2, 2, 128, 128), (1, 2, 2, 128, 128)]


def constants():
    t = np.arange(P)
    half = 32
    freqs = (np.float32(10000.0) ** (-np.arange(half, dtype=np.float32) / np.float32(half))).astype(np.float32)
    rope = np.zeros((P, 2, 2, 2, half), np.float32)
    for axis, pos in enumerate((t // GRID, t % GRID)):
        ang = pos.astype(np.float32)[:, None] * freqs[None, :]
        rope[:, 0, axis, 0] = rope[:, 0, axis, 1] = np.cos(ang)
        rope[:, 1, axis, 0] = -np.sin(ang)
        rope[:, 1, axis, 1] = np.sin(ang)
    col = t % GRID
    c0 = np.clip(col - 8, 0, GRID - 16)
    ok = (col[None, :] >= c0[:, None]) & (col[None, :] < c0[:, None] + 16)
    rsel = np.zeros((P, 2), np.float32)
    rsel[0::32, 0] = rsel[1::32, 1] = 1
    return {
        "c_ident": np.eye(P, dtype=np.float32), "c_rsel": rsel, "c_rope": rope.reshape(P, 2 * P),
        "c_edge": np.where(ok, 0, NEG).astype(np.float32),
        "c_zero": np.zeros((DEPTH * NH * 3, 2 * GRID - 1), np.float32),
    }


def kernel(**inputs):
    import concourse.bacc as bacc
    from concourse.bass_utils import run_bass_kernel_spmd

    nc = bacc.Bacc("TRN2", target_bir_lowering=False, num_devices=1)
    arrays, args = {}, {}
    for name, v in [(n, inputs[n]) for n in _INS] + list(constants().items()):
        v = np.ascontiguousarray(v)
        arrays[f"in_{name}"] = v
        args[name] = nc.dram_tensor(f"in_{name}", v.shape, F32, kind="ExternalInput").ap()
    for i, shape in enumerate(_OUTS):
        args[f"out_{i}"] = nc.dram_tensor(f"out_{i}", shape, F32, kind="ExternalOutput").ap()
    build_program(nc, args)
    r = run_bass_kernel_spmd(nc, [arrays], core_ids=[0])
    return tuple(r.results[0][f"out_{i}"] for i in range(len(_OUTS)))
```
